# Optimizing a Trainium2 kernel written in Bass

```python
import math
import jax, jax.numpy as jnp
from jax import lax
import numpy as np

D_MODEL = 1024
BATCH = 1
SEQ = 1024
DEPTH = 1
DEC_BATCH = 8
DEC_SEQ = 8
PAST_LEN = 8192
PAGE_SIZE = 128

H_A = 4
DK_A = D_MODEL // 16
DV_A = D_MODEL // 8
GATE_RANK = 16
GATE_NORM = 16.0
H_B = 4
DK_B = D_MODEL // 8
DV_B = D_MODEL // 8
D_FF = -(-8 * D_MODEL // (3 * 256)) * 256
CHUNK = 32
EPS = 1e-6
SPLIT_SIZES = (H_A * DK_A, H_A * DK_A, H_A * DV_A, H_A * DV_A, GATE_RANK,
               H_B * DK_B, H_B * DK_B, H_B * DV_B, H_B * DV_B)
D_IN = sum(SPLIT_SIZES)

kernel_name = "hymba_gla_hgrn2_step"

def rmsnorm(x, g):
    xf = x.astype(jnp.float32)
    y = xf * lax.rsqrt(jnp.mean(xf * xf, axis=-1, keepdims=True) + EPS) * g.astype(jnp.float32)
    return y.astype(x.dtype)

def head_rmsnorm(o, g):
    return o * lax.rsqrt(jnp.mean(o * o, axis=-1, keepdims=True) + EPS) * g.astype(jnp.float32)

def chunk_gated_linear(q, k, v, log_a, s0):
    B, T, H, K = q.shape
    n = -(-T // CHUNK)
    pad = n * CHUNK - T
    f32 = jnp.float32
    q, k, v, log_a = (t.astype(f32) for t in (q, k, v, log_a))
    if pad:
        pw = ((0, 0), (0, pad), (0, 0), (0, 0))
        q, k, v, log_a = (jnp.pad(t, pw) for t in (q, k, v, log_a))

    def to_chunks(t):
        return t.reshape(B, n, CHUNK, H, t.shape[-1]).transpose(1, 0, 3, 2, 4)

    qc, kc, vc = to_chunks(q), to_chunks(k), to_chunks(v)
    bc = jnp.cumsum(to_chunks(log_a), axis=3)
    mask = jnp.tril(jnp.ones((CHUNK, CHUNK), dtype=bool))

    def step(S, xs):
        qi, ki, vi, bi = xs
        q_in = qi * jnp.exp(bi)
        k_in = ki * jnp.exp(-bi)
        att = jnp.where(mask, jnp.einsum('bhtk,bhsk->bhts', q_in, k_in), 0.0)
        o = jnp.einsum('bhtk,bhkv->bhtv', q_in, S) + jnp.einsum('bhts,bhsv->bhtv', att, vi)
        b_last = bi[:, :, -1:, :]
        S = jnp.exp(b_last[:, :, 0, :])[..., None] * S + jnp.einsum(
            'bhsk,bhsv->bhkv', ki * jnp.exp(b_last - bi), vi)
        return S, o

    S, o = lax.scan(step, s0.astype(f32), (qc, kc, vc, bc))
    o = o.transpose(1, 0, 3, 2, 4).reshape(B, n * CHUNK, H, -1)[:, :T]
    return o, S

def mixer(h, s_gla, s_hgrn, w_in, w_a2, b_a, lb, onorm_a, onorm_b, w_o):
    B, T, _ = h.shape
    idx, acc = [], 0
    for s in SPLIT_SIZES[:-1]:
        acc += s
        idx.append(acc)
    p = h @ w_in
    qa, ka, va, ga, lra, qb, fb, ib, gb = jnp.split(p.astype(jnp.float32), idx, axis=-1)

    qa = qa.reshape(B, T, H_A, DK_A) * (DK_A ** -0.5)
    ka = ka.reshape(B, T, H_A, DK_A)
    va = va.reshape(B, T, H_A, DV_A)
    log_alpha = jax.nn.log_sigmoid(lra @ w_a2.astype(jnp.float32) + b_a.astype(jnp.float32)) / GATE_NORM
    log_alpha = log_alpha.reshape(B, T, H_A, DK_A)
    oa, sa = chunk_gated_linear(qa, ka, va, log_alpha, s_gla)
    oa = head_rmsnorm(oa, onorm_a) * jax.nn.silu(ga.reshape(B, T, H_A, DV_A))

    qb = jax.nn.silu(qb.reshape(B, T, H_B, DK_B))
    f = lb + (1.0 - lb) * jax.nn.sigmoid(fb.reshape(B, T, H_B, DK_B))
    kb = 1.0 - f
    ib = ib.reshape(B, T, H_B, DV_B)
    ob, sb = chunk_gated_linear(qb, kb, ib, jnp.log(f), s_hgrn)
    ob = head_rmsnorm(ob, onorm_b) * jax.nn.silu(gb.reshape(B, T, H_B, DV_B))

    o = jnp.concatenate([oa.reshape(B, T, H_A * DV_A), ob.reshape(B, T, H_B * DV_B)], axis=-1)
    return o.astype(h.dtype) @ w_o, sa, sb

def swiglu(h, w1, w3, w2):
    return (jax.nn.silu(h @ w1) * (h @ w3)) @ w2

def trunk(x, s_gla, s_hgrn, norm_mix, w_in, w_a2, b_a, lb_all, onorm_a, onorm_b, w_o,
          norm_ffn, w1, w3, w2, norm_final):
    sa_list, sb_list = [], []
    for l in range(DEPTH):
        lb = lb_all[l].reshape(H_B, DK_B)
        m, sa, sb = mixer(rmsnorm(x, norm_mix[l]), s_gla[l], s_hgrn[l], w_in[l], w_a2[l], b_a[l],
                          lb, onorm_a[l], onorm_b[l], w_o[l])
        x = x + m
        x = x + swiglu(rmsnorm(x, norm_ffn[l]), w1[l], w3[l], w2[l])
        sa_list.append(sa)
        sb_list.append(sb)
    return rmsnorm(x, norm_final), jnp.stack(sa_list), jnp.stack(sb_list)

def setup_inputs(seed: int = 0) -> dict:
    key = jax.random.key(seed)
    ks = jax.random.split(key, 20)
    f32 = jnp.float32
    nrm = lambda k, shape, s: jax.random.normal(k, shape, f32) * s
    return {
        "x_prompt": nrm(ks[0], (BATCH, SEQ, D_MODEL), 1.0),
        "x_sample": nrm(ks[1], (DEC_BATCH, DEC_SEQ, D_MODEL), 1.0),
        "state_gla": nrm(ks[2], (DEPTH, DEC_BATCH, H_A, DK_A, DV_A), 2.0),
        "state_hgrn": nrm(ks[3], (DEPTH, DEC_BATCH, H_B, DK_B, DV_B), 0.5),
        "norm_mix": 1.0 + nrm(ks[4], (DEPTH, D_MODEL), 0.02),
        "w_in": nrm(ks[5], (DEPTH, D_MODEL, D_IN), D_MODEL ** -0.5),
        "w_a2": nrm(ks[6], (DEPTH, GATE_RANK, H_A * DK_A), GATE_RANK ** -0.5),
        "b_a": nrm(ks[7], (DEPTH, H_A * DK_A), 0.01),
        "lb_param": nrm(ks[8], (DEPTH + 1, H_B * DK_B), 1.0),
        "onorm_a": 1.0 + nrm(ks[9], (DEPTH, DV_A), 0.02),
        "onorm_b": 1.0 + nrm(ks[10], (DEPTH, DV_B), 0.02),
        "w_o": nrm(ks[11], (DEPTH, D_MODEL, D_MODEL), D_MODEL ** -0.5),
        "norm_ffn": 1.0 + nrm(ks[12], (DEPTH, D_MODEL), 0.02),
        "w1": nrm(ks[13], (DEPTH, D_MODEL, D_FF), D_MODEL ** -0.5),
        "w3": nrm(ks[14], (DEPTH, D_MODEL, D_FF), D_MODEL ** -0.5),
        "w2": nrm(ks[15], (DEPTH, D_FF, D_MODEL), D_FF ** -0.5),
        "norm_final": 1.0 + nrm(ks[16], (D_MODEL,), 0.02),
    }

def reference(x_prompt, x_sample, state_gla, state_hgrn, norm_mix, w_in, w_a2, b_a, lb_param,
              onorm_a, onorm_b, w_o, norm_ffn, w1, w3, w2, norm_final):
    lb_all = jnp.cumsum(jax.nn.softmax(lb_param.astype(jnp.float32), axis=0), axis=0)
    zeros_a = jnp.zeros((DEPTH, BATCH, H_A, DK_A, DV_A), jnp.float32)
    zeros_b = jnp.zeros((DEPTH, BATCH, H_B, DK_B, DV_B), jnp.float32)
    weights = (norm_mix, w_in, w_a2, b_a, lb_all, onorm_a, onorm_b, w_o, norm_ffn, w1, w3, w2, norm_final)
    y_prompt, sa_p, sb_p = trunk(x_prompt, zeros_a, zeros_b, *weights)
    y_sample, sa_s, sb_s = trunk(x_sample, state_gla, state_hgrn, *weights)
    return (y_prompt, y_sample, sa_p, sb_p, sa_s, sb_s)


_drawn_inputs = setup_inputs


def setup_inputs(seed=0):
    import zlib

    import numpy as np

    out = dict(_drawn_inputs(seed))
    spreads = {}
    factors = {'b_a': 8.0, 'onorm_a': 6.138, 'onorm_b': 6.118, 'norm_ffn': 4.385, 'norm_final': 2.863}
    for name, (base, spread) in spreads.items():
        noise = np.random.default_rng([zlib.crc32(name.encode()), seed]).standard_normal(out[name].shape)
        drawn = base * np.exp(spread * noise) if base else spread * noise
        out[name] = __import__('jax').numpy.asarray(drawn.astype(out[name].dtype))
    for name, factor in factors.items():
        out[name] = (out[name] * factor).astype(out[name].dtype)
    return out
```

```python
from contextlib import ExitStack

import concourse.bass as bass
from concourse import mybir

F32 = mybir.dt.float32
F32R = mybir.dt.float32r
U32 = mybir.dt.uint32
ACT = mybir.ActivationFunctionType
ALU = mybir.AluOpType

P = 128
D = 1024
KT_D = D // P
SEQ = 1024
HALF = 512
SB, ST = 8, 8
NS = SB * ST
NTOK = SEQ + NS
HA, KA = 4, 64
HB = 4
NH = HA + HB
V = 128
RANK = 16
SLOTS = HA // 2 + HB
DFF = 2816
GROUPS = DFF // 256
CH = 32
SC = 128
NSC = HALF // SC
NCH = SC // CH
EPS = 1e-6
GATE_NORM = 16.0

A_UNITS, V_UNITS, O_UNITS = 10, 4, 4
L_UNIT = A_UNITS
V0_UNIT = L_UNIT + 1
O0_UNIT = V0_UNIT + V_UNITS
HALF_UNITS = O0_UNIT + O_UNITS
F0_UNIT = 2 * HALF_UNITS
A_TILES = 2 * A_UNITS
QT, KTL, GT = 0, SLOTS, 2 * SLOTS
FT = KTL + HA // 2

C_ID, C_ONE, C_CAUSAL = 0, 128, 256
C_M32 = 384
C_M8 = C_M32 + SLOTS * SC
C_SMASK = C_M8 + SLOTS * NS
C_BMASK = C_SMASK + NS
C_ALL = C_BMASK + SB
V_GMIX, V_GFFN, V_BA, V_LB, V_ONA, V_ONB, V_ALL = 0, 8, 16, 18, 26, 27, 28

PLACE = [4, 5, 6, 7, 0, 1, 2, 3, 8]
FF_CHUNKS = [(0, 384), (384, 384), (768, 320)]


def half_tiles(h):
    tiles = [(PLACE[4 * h + j], P, j * P) for j in range(4)]
    return tiles + [(8, NS, HALF)] if h == 0 else tiles


ORDER = [0, 2, 4, 5, 1, 3, 6, 7]


def head_place(n):
    return (n // 2, KA * (n % 2), KA) if n < HA else (n - HA + HA // 2, 0, P)


def build(nc, x_prompt, x_sample, state_gla, state_hgrn, wstream_a, wstream_l, wstream_b, wstream_f,
          consts, pvec, w_a2, norm_final,
          y_prompt, y_sample, new_gla_p, new_hgrn_p, new_gla_s, new_hgrn_s):
    with ExitStack() as ctx:
        def sem(name):
            return ctx.enter_context(nc.semaphore(name))

        def tensor(scope, name, shape, dt=F32):
            return scope.enter_context(nc.sbuf_tensor(name, shape, dt))

        con = tensor(ctx, "con", [P, C_ALL])
        pv = tensor(ctx, "pv", [P, V_ALL])
        wa2 = tensor(ctx, "wa2", [RANK, HA * KA])
        x_res = tensor(ctx, "x_res", [P, 9, D])
        raw0 = tensor(ctx, "raw0", [P, 2048])
        whi = [tensor(ctx, f"whi{s}", [P, 2048], F32R) for s in range(2)]
        wlo = [tensor(ctx, f"wlo{s}", [P, 2048], F32R) for s in range(2)]
        small = tensor(ctx, "small", [P, 88])
        ms = small[:, 0:9]
        rs = small[:, 9:18]
        lb = small[:, 18:22]
        omlb = small[:, 22:26]
        lbw = small[:, 26:38].rearrange("p (a b) -> p a b", a=3)
        eps_t = small[:, 38:39]

        mix = ExitStack()
        p_main = tensor(mix, "p_main", [P, NSC, A_TILES, SC])
        p_samp = tensor(mix, "p_samp", [P, A_TILES, NS])
        b_main = tensor(mix, "b_main", [P, NSC, SLOTS, SC])
        b_samp = tensor(mix, "b_samp", [P, SLOTS, NS])
        val = tensor(mix, "val", [P, 5, NH * V])
        att = tensor(mix, "att", [P, 2, 4, SC])
        state = tensor(mix, "state", [P, SLOTS, V])
        fac = tensor(mix, "fac", [P, 2, SLOTS, 4 + 4 + 2 + 2 + 1 + 4])
        hscope = ExitStack()
        h_hi = tensor(hscope, "h_hi", [P, KT_D, HALF + NS], F32R)
        h_lo = tensor(hscope, "h_lo", [P, KT_D, HALF + NS], F32R)
        hscope.close()
        tscope = ExitStack()
        q_in, k_in, k_out, q_st, q_64, k_64 = [], [], [], [], [], []
        for j in range(2):
            for name, bufs, width in (("q_in", q_in, SC), ("k_in", k_in, SC), ("k_out", k_out, SC),
                                      ("q_st", q_st, SC), ("q_64", q_64, SC // 2), ("k_64", k_64, SC // 2)):
                bufs.append(tensor(tscope, f"{name}{j}", [P, SLOTS, width]))
        k_st = tensor(tscope, "k_st", [P, SLOTS, SC])
        kT_st = tensor(tscope, "kT_st", [P, SLOTS, SC])
        tscope.close()
        sscope = ExitStack()
        sq_in = tensor(sscope, "sq_in", [P, SLOTS, NS])
        sk_in = tensor(sscope, "sk_in", [P, SLOTS, NS])
        sk_out = tensor(sscope, "sk_out", [P, SLOTS, NS])
        skT = [tensor(sscope, f"skT{j}", [NS, SB, P]) for j in range(2)]
        s_att = tensor(sscope, "s_att", [P, NH, NS])
        sscope.close()
        mix.close()

        ffn = ExitStack()
        f_hi = tensor(ffn, "f_hi", [P, KT_D, NTOK], F32R)
        f_lo = tensor(ffn, "f_lo", [P, KT_D, NTOK], F32R)
        raw1 = tensor(ffn, "raw1", [P, 2048])
        whi.append(tensor(ffn, "whi2", [P, 2048], F32R))
        wlo.append(tensor(ffn, "wlo2", [P, 2048], F32R))
        gated = tensor(ffn, "gated", [P, 2, 384])
        nf = tensor(ffn, "nf", [P, D])
        xscope = ExitStack()
        f_xn = tensor(xscope, "f_xn", [P, 4, D])
        xscope.close()
        g_hi = tensor(ffn, "g_hi", [P, 2, NTOK], F32R)
        g_lo = tensor(ffn, "g_lo", [P, 2, NTOK], F32R)
        ffn.close()

        lr_t = [x_res[0:RANK, 6, 0:HALF + NS], val[0:RANK, 4, 0:HALF]]
        az_s = x_res[:, 7, 0:2 * NS].rearrange("p (a t) -> p a t", a=2)
        az_m = att[:].rearrange("p g n t -> p (g n t)").rearrange("p (c a t) -> p c a t", c=NSC, a=2)
        s_state = x_res[:, 0:6, :].rearrange("p a d -> p (a d)").rearrange(
            "p (b s v) -> p b s v", b=SB, s=SLOTS)

        ps = ctx.enter_context(nc.psum_tensor("ps", [P, 8, 512], F32))

        ident = con[:, C_ID:C_ID + P]
        ones = con[:, C_ONE:C_ONE + P]
        causal = con[:, C_CAUSAL:C_CAUSAL + P].bitcast(U32)
        m32 = con[:, C_M32:C_M32 + SLOTS * SC]
        m8 = con[:, C_M8:C_M8 + SLOTS * NS]
        smask = con[0:NS, C_SMASK:C_SMASK + NS].bitcast(U32)
        bmask = con[0:NS, C_BMASK:C_BMASK + SB]
        fq = [fac[:, j, :, 0:4] for j in range(2)]
        gk = [fac[:, j, :, 4:8] for j in range(2)]
        f64 = [fac[:, j, :, 8:10] for j in range(2)]
        g64 = [fac[:, j, :, 10:12] for j in range(2)]
        dtot = [fac[:, j, :, 12:13] for j in range(2)]
        ech = [fac[:, j, :, 13:17] for j in range(2)]
        dsamp = small[:, 39:39 + SLOTS * SB].rearrange("p (s b) -> p s b", s=SLOTS)

        c_ld = sem("consts_loaded")
        x_ld = [sem("x_loaded0"), sem("x_loaded1")]
        xr_ld = sem("x_reloaded")
        raw0_ld, raw1_ld = sem("raw0_loaded"), sem("raw1_loaded")
        st_ld = sem("sample_states_loaded")
        nf_ld = sem("norm_final_loaded")
        out_st = sem("outputs_stored")
        lb_e, lb_v = sem("lb_exp"), sem("lb_vector")
        eps_set = sem("eps_set")
        sq_done, rms_done = sem("squares_done"), sem("rms_done")
        rs_done, xn_done = sem("rstd_done"), sem("xn_done")
        tr_done, th_done, tl_done = sem("transposed"), sem("hT_hi_done"), sem("hT_lo_done")
        hi_done, lo_done, used = sem("weights_hi"), sem("weights_lo"), sem("unit_used")
        ev_a, ev_v = sem("unit_evacuated_act"), sem("unit_evacuated_dve")
        lr_done, z_pe, z_dve = sem("low_rank_copied"), sem("z_product"), sem("z_biased")
        silu_done, sig_done, f_done, lnf_done, k_done = (
            sem("silu_done"), sem("sigmoid_done"), sem("forget_done"), sem("log_forget_done"), sem("k_done"))
        az_done, aze_done, azl_done, zm_done, la_done = (
            sem("abs_z_done"), sem("exp_abs_z"), sem("ln1p_done"), sem("min_z_done"), sem("log_alpha_done"))
        la2_done, b_done, g_done, qs_done = sem("log_decay_done"), sem("cumsum_done"), sem("gate_scaled"), sem("q_scaled")
        zero_att, zero_state, ones_fac = sem("att_zeroed"), sem("state_zeroed"), sem("factors_set")
        e1_done, e3_done = sem("exp_b_done"), sem("exp_d_done")
        d_done, prep1_done, prep_done = sem("d_done"), sem("q_k_decayed"), sem("prep_done")
        fac_a, fac_b, pool_q, pool_k = sem("factors_a"), sem("factors_b"), sem("pool_q_done"), sem("pool_k_done")
        kt_pe, kt_act = sem("k_transposed"), sem("kT_copied")
        att_pe, att_dve = sem("scores_done"), sem("scores_masked")
        kv_pe, st_done = sem("kv_done"), sem("state_updated")
        o_pe, o_act, osq_act = sem("o_done"), sem("o_copied"), sem("o_squared")
        ss_pe, ln_act, rn_act = sem("sumsq_done"), sem("ln_ms_done"), sem("rstd_o_done")
        on_dve, og_pool = sem("o_normed"), sem("o_gated")
        oh_act, ol_dve = sem("oT_hi_done"), sem("oT_lo_done")
        s_b, s_e1, s_d, s_e3, s_prep = sem("s_cumsum"), sem("s_exp_b"), sem("s_d"), sem("s_exp_d"), sem("s_prep")
        s_zero, s_att_pe, s_att_dve = sem("s_att_zeroed"), sem("s_scores_done"), sem("s_scores_masked")
        s_t, s_dm, s_kv = sem("s_transposed"), sem("s_kT_masked"), sem("s_kv_done")
        s_decayed, s_upd = sem("s_state_decayed"), sem("s_state_updated")
        s_o, s_ocp, s_osq, s_ss = sem("s_o_done"), sem("s_o_copied"), sem("s_o_squared"), sem("s_sumsq_done")
        s_ln, s_rn, s_on, s_og = sem("s_ln_ms_done"), sem("s_rstd_o_done"), sem("s_o_normed"), sem("s_o_gated")
        z_s_pe, z_s_dve = sem("s_z_product"), sem("s_z_biased")
        step_pe, silu_f, gm_done, gh_done, gl_done = (
            sem("ffn_step_done"), sem("ffn_silu"), sem("ffn_gated"), sem("ffn_g_hi"), sem("ffn_g_lo"))
        y_pe, y_dve = sem("ffn_out_done"), sem("ffn_out_added")
        fx_done, sqf, rmsf, rsf, yf_done = (
            sem("ffn_xn_done"), sem("final_squares"), sem("final_rms"), sem("final_rstd"), sem("final_y"))

        block = ctx.enter_context(nc.Block())

        def half(h, size=NS):
            return size if h == 0 else 0

        @block.sync
        def _(sp):
            sp.dma_start(con[:], consts).then_inc(c_ld, 16)
            sp.dma_start(pv[:], pvec).then_inc(c_ld, 16)
            sp.dma_start(wa2[:], w_a2).then_inc(c_ld, 16)

            def load_x(h):
                for j in range(4):
                    t = 4 * h + j
                    sp.dma_start(x_res[:, PLACE[t], :], x_prompt[t * P:(t + 1) * P, :]).then_inc(x_ld[h], 16)

            load_x(0)
            sp.dma_start(x_res[0:NS, 8, :], x_sample).then_inc(x_ld[0], 16)

            def load_unit(u, src, size=2048):
                if u:
                    sp.wait_ge(lo_done, u)
                sp.dma_start(raw0[:, 0:size], src).then_inc(raw0_ld, 16)

            def sample_states():
                sp.wait_ge(xn_done, 5)
                for p in range(2):
                    for e in range(2):
                        sp.dma_start(s_state[KA * e:KA * (e + 1), :, p, :],
                                     state_gla[:, 2 * p + e].rearrange("b k v -> k b v")).then_inc(st_ld, 16)
                for n in range(HB):
                    sp.dma_start(s_state[:, :, 2 + n, :],
                                 state_hgrn[:, n].rearrange("b k v -> k b v")).then_inc(st_ld, 16)

            def store_sample_states():
                for n in range(NH):
                    slot, lo, kw = head_place(n)
                    sp.wait_ge(s_upd, slot + 1)
                    dst = new_gla_s[:, n] if n < HA else new_hgrn_s[:, n - HA]
                    sp.dma_start(dst.rearrange("b k v -> k b v"),
                                 s_state[lo:lo + kw, :, slot, :]).then_inc(out_st, 16)

            for h in range(2):
                u0 = h * HALF_UNITS
                for r in range(O0_UNIT):
                    u = u0 + r
                    if r < A_UNITS:
                        load_unit(u, wstream_a[r])
                    elif r == L_UNIT:
                        load_unit(u, wstream_l, 1024)
                    else:
                        load_unit(u, wstream_b[r - V0_UNIT])
                    if h == 0 and r == 3:
                        sample_states()
                for r in range(2):
                    load_unit(u0 + O0_UNIT + r, wstream_b[V_UNITS + r])
                if h == 0:
                    store_sample_states()
                    sp.wait_ge(out_st, 16 * NH)
                    for t in range(4):
                        sp.dma_start(x_res[:, PLACE[t], :], x_prompt[t * P:(t + 1) * P, :]).then_inc(xr_ld, 16)
                    load_x(1)
                else:
                    sp.wait_ge(st_done, 2 * NSC)
                    for p in range(2):
                        for e in range(2):
                            sp.dma_start(new_gla_p[2 * p + e],
                                         state[KA * e:KA * (e + 1), p, :]).then_inc(out_st, 16)
                    for n in range(HB):
                        sp.dma_start(new_hgrn_p[n], state[:, 2 + n, :]).then_inc(out_st, 16)
                for r in range(2, O_UNITS):
                    load_unit(u0 + O0_UNIT + r, wstream_b[V_UNITS + r])

            sp.wait_ge(lo_done, F0_UNIT)
            sp.dma_start(raw0[:], wstream_f[0]).then_inc(raw0_ld, 16)
            sp.wait_ge(used, F0_UNIT)
            sp.wait_ge(out_st, 2 * 16 * NH)
            sp.dma_start(raw1[:], wstream_f[1]).then_inc(raw1_ld, 16)
            sp.dma_start(nf[:], norm_final.partition_broadcast(P)).then_inc(nf_ld, 16)
            sp.wait_ge(lo_done, F0_UNIT + 1)
            sp.dma_start(raw0[:], wstream_f[2]).then_inc(raw0_ld, 16)
            with sp.Fori(1, GROUPS) as i:
                sp.wait_ge(lo_done, i * 3 + F0_UNIT)
                sp.dma_start(raw0[:], wstream_f[bass.ds(i * 3, 1)].rearrange("u p c -> p (u c)")).then_inc(raw0_ld, 16)
                sp.dma_start(raw1[:], wstream_f[bass.ds(i * 3 + 1, 1)].rearrange("u p c -> p (u c)")).then_inc(raw1_ld, 16)
                sp.wait_ge(lo_done, i * 3 + F0_UNIT + 1)
                sp.dma_start(raw0[:], wstream_f[bass.ds(i * 3 + 2, 1)].rearrange("u p c -> p (u c)")).then_inc(raw0_ld, 16)
            for t in range(9):
                sp.wait_ge(yf_done, t + 1)
                if t < 8:
                    sp.dma_start(y_prompt[t * P:(t + 1) * P, :], x_res[:, PLACE[t], :]).then_inc(out_st, 16)
                else:
                    sp.dma_start(y_sample, x_res[0:NS, 8, :]).then_inc(out_st, 16)
            sp.wait_ge(out_st, 2 * 16 * NH + 16 * 9)

        @block.gpsimd
        def _(pool):
            nc.gpsimd.memset(eps_t, EPS).then_inc(eps_set, 1)
            nc.gpsimd.memset(fac[:], 1.0).then_inc(ones_fac, 1)
            nc.gpsimd.memset(state[:], 0.0).then_inc(zero_state, 1)
            for h in range(2):
                pool.wait_ge(la_done, h + 1)
                nc.gpsimd.memset(att[:], 0.0).then_inc(zero_att, 1)

                def gate(C):
                    c = C % NSC
                    pool.wait_ge(on_dve, 2 * (C + 1))
                    o = p_main[:, c, 0:NH, :]
                    nc.gpsimd.tensor_tensor(o, o, p_main[:, c, GT:GT + NH, :], ALU.mult).then_inc(og_pool, 1)

                for c in range(NSC):
                    C = NSC * h + c
                    j = C % 2
                    pool.wait_ge(e1_done, 3 * (C + 1))
                    if C == 0:
                        pool.wait_ge(ones_fac, 1)
                    if C >= 2:
                        pool.wait_ge(st_done, C - 1)
                        pool.wait_ge(prep_done, C - 1)
                        pool.wait_ge(pool_k, C - 1)
                        pool.wait_ge(pool_q, C - 1)
                    nc.gpsimd.tensor_copy(fq[j][:, :, 1:2], ech[j][:, :, 0:1])
                    nc.gpsimd.tensor_tensor(fq[j][:, :, 2:3], ech[j][:, :, 0:1], ech[j][:, :, 1:2], ALU.mult)
                    nc.gpsimd.tensor_copy(gk[j][:, :, 2:3], ech[j][:, :, 3:4])
                    nc.gpsimd.tensor_tensor(gk[j][:, :, 1:2], ech[j][:, :, 3:4], ech[j][:, :, 2:3], ALU.mult)
                    nc.gpsimd.tensor_copy(g64[j][:, :, 0:1], ech[j][:, :, 1:2])
                    nc.gpsimd.tensor_copy(f64[j][:, :, 1:2], ech[j][:, :, 2:3]).then_inc(fac_a, 1)
                    pool.wait_ge(fac_a, C + 1)
                    nc.gpsimd.tensor_tensor(fq[j][:, :, 3:4], fq[j][:, :, 2:3], ech[j][:, :, 2:3], ALU.mult)
                    nc.gpsimd.tensor_tensor(gk[j][:, :, 0:1], gk[j][:, :, 1:2], ech[j][:, :, 1:2], ALU.mult)
                    nc.gpsimd.tensor_tensor(dtot[j], fq[j][:, :, 2:3], gk[j][:, :, 1:2], ALU.mult).then_inc(fac_b, 1)
                    pool.wait_ge(fac_b, C + 1)
                    pool.wait_ge(prep1_done, C + 1)
                    if C >= 1:
                        pool.wait_ge(kt_pe, C)
                    nc.gpsimd.tensor_tensor(
                        k_st[:].rearrange("p s (c t) -> p s c t", c=NCH),
                        k_out[j][:].rearrange("p s (c t) -> p s c t", c=NCH),
                        gk[j].unsqueeze(3).broadcast_to((P, SLOTS, NCH, CH)), ALU.mult).then_inc(pool_k, 1)
                    if C >= 2:
                        pool.wait_ge(o_pe, 2 * (C - 1))
                    nc.gpsimd.tensor_tensor(
                        q_st[j][:].rearrange("p s (c t) -> p s c t", c=NCH),
                        q_in[j][:].rearrange("p s (c t) -> p s c t", c=NCH),
                        fq[j].unsqueeze(3).broadcast_to((P, SLOTS, NCH, CH)), ALU.mult).then_inc(pool_q, 1)
                    if c >= 2:
                        gate(C - 2)
                if h == 0:
                    pool.wait_ge(o_pe, 2 * 3)
                    nc.gpsimd.memset(s_att[:], 0.0).then_inc(s_zero, 1)
                gate(NSC * h + 2)
                gate(NSC * h + 3)
                if h == 0:
                    pool.wait_ge(s_o, 1)
                    pool.wait_ge(s_e1, 3)
                    for slot in range(SLOTS):
                        st = s_state[:, :, slot, :]
                        nc.gpsimd.tensor_tensor(st, st, dsamp[:, slot, :].unsqueeze(2).broadcast_to((P, SB, V)),
                                                ALU.mult).then_inc(s_decayed, 1)
                        if slot == 2:
                            pool.wait_ge(s_on, 1)
                            nc.gpsimd.tensor_tensor(p_samp[:, 0:NH, :], p_samp[:, 0:NH, :],
                                                    p_samp[:, GT:GT + NH, :], ALU.mult).then_inc(s_og, 1)

        def stage_parts(n):
            if n < 2:
                first = PLACE[4 * n]
                main = [(first + j, P, val[:, j, :]) for j in range(4)]
                samp = (8, NS, val[0:NS, 4, :]) if n == 0 else None
                return main, samp, h_hi, h_lo, 0, HALF, V_GMIX
            if n < 4:
                first = PLACE[4 * (n - 2)]
                main = [(first + j, P, f_xn[:, j, :]) for j in range(4)]
                return main, None, f_hi, f_lo, HALF * (n - 2), None, V_GFFN
            return [], (8, NS, f_xn[0:NS, 0, :]), f_hi, f_lo, None, SEQ, V_GFFN

        N_STAGES = 5

        def tiles_before(n):
            return sum(len(stage_parts(m)[0]) + bool(stage_parts(m)[1]) for m in range(n))

        def turns_before(n):
            return sum(KT_D * bool(stage_parts(m)[0]) + bool(stage_parts(m)[1]) for m in range(n))

        def groups_before(n):
            return sum(bool(stage_parts(m)[0]) + bool(stage_parts(m)[1]) for m in range(n))

        def row_groups(n):
            main, samp = stage_parts(n)[:2]
            return ([(main[0][0], 4, P)] if main else []) + ([(8, 1, NS)] if samp else [])

        def act_copies_before(u):
            h, r = divmod(u, HALF_UNITS)
            return O0_UNIT * h + min(r, O0_UNIT)

        def slot_of(u):
            return u % 2 if u < F0_UNIT else (u - F0_UNIT) % 3

        def sum_place(C, g, samp=False):
            if samp:
                return p_samp[:, KTL + 2:KTL + 6, :] if g == 0 else b_samp[:, 0:4, :]
            c = C % NSC
            return p_main[:, c, KTL + 2:KTL + 6, :] if g == 0 else b_main[:, c, 0:4, :]

        @block.scalar
        def _(act):
            def split_hi(u):
                size = 1024 if u % HALF_UNITS == L_UNIT else 2048
                act.wait_ge(raw0_ld, 16 * (u + 1))
                if u >= 2:
                    act.wait_ge(used, u - 1)
                s = slot_of(u)
                nc.scalar.activation(whi[s][:, 0:size], raw0[:, 0:size], ACT.Copy).then_inc(hi_done, 1)

            def norm(n):
                main, samp, hi, lo, mcol, scol, gain = stage_parts(n)
                if n == 0:
                    act.wait_ge(eps_set, 1)
                if n < 2:
                    act.wait_ge(x_ld[n], 16 * (4 + (n == 0)))
                else:
                    act.wait_ge(ev_v, F0_UNIT + 2)
                cnt = tiles_before(n)
                for place, rows, scratch in main + ([samp] if samp else []):
                    if n == 1:
                        act.wait_ge(o_pe, 2 * NSC)
                        act.wait_ge(s_kv, SLOTS)
                    if n >= 2:
                        act.wait_ge(out_st, 2 * 16 * NH)
                        act.wait_ge(used, F0_UNIT)
                    if n >= 3:
                        act.wait_ge(tr_done, turns_before(n))
                    nc.scalar.activation(scratch, x_res[0:rows, place, :], ACT.Square,
                                         accum_out=ms[0:rows, place:place + 1]).then_inc(sq_done, 1)
                for m, (place, num, rows) in enumerate(row_groups(n)):
                    act.wait_ge(sq_done, cnt + (num if m == 0 else tiles_before(n + 1) - cnt))
                    col = ms[0:rows, place:place + num]
                    nc.scalar.activation(col, col, ACT.Sqrt, scale=1.0 / D, bias=eps_t[0:rows]).then_inc(rms_done, 1)
                t0 = turns_before(n)
                if main:
                    for k in range(KT_D):
                        act.wait_ge(tr_done, t0 + k + 1)
                        nc.scalar.activation(hi[:, k, mcol:mcol + HALF], ps[:, k % 4, :], ACT.Copy,
                                             scale=pv[:, gain + k:gain + k + 1]).then_inc(th_done, 1)
                if samp:
                    act.wait_ge(tr_done, turns_before(n + 1))
                    for k in range(KT_D):
                        last = nc.scalar.activation(hi[:, k, scol:scol + NS], ps[:, 4, k * NS:(k + 1) * NS],
                                                    ACT.Copy, scale=pv[:, gain + k:gain + k + 1])
                    last.then_inc(th_done, 1)

            def exps(C):
                c, j = C % NSC, C % 2
                act.wait_ge(b_done, C + 1)
                act.wait_ge(used, HALF_UNITS * (C // NSC) + O0_UNIT)
                if C == 0:
                    act.wait_ge(ones_fac, 1)
                if C >= 2:
                    act.wait_ge(o_pe, 2 * (C - 1))
                    act.wait_ge(pool_q, C - 1)
                    act.wait_ge(fac_b, C - 1)
                if C == NSC:
                    act.wait_ge(ol_dve, KT_D)
                b = b_main[:, c]
                ends = b.rearrange("p s (c t) -> p s c t", c=NCH)[:, :, :, CH - 1:CH]
                nc.scalar.activation(q_in[j][:], b, ACT.Exp).then_inc(e1_done, 1)
                nc.scalar.activation(k_in[j][:], b, ACT.Exp, scale=-1.0).then_inc(e1_done, 1)
                nc.scalar.activation(ech[j].unsqueeze(3), ends, ACT.Exp).then_inc(e1_done, 1)

            def exp_d(C):
                j = C % 2
                act.wait_ge(d_done, C + 1)
                nc.scalar.activation(k_out[j][:], k_out[j][:], ACT.Exp).then_inc(e3_done, 1)

            def rstd(C, g, bank, count, ln_sem, rn_sem, width, samp=False):
                place = sum_place(C, g, samp)
                nc.scalar.activation(place, bank, ACT.Ln, scale=1.0 / V, bias=eps_t).then_inc(ln_sem, 1)
                act.wait_ge(ln_sem, count)
                nc.scalar.activation(place, place, ACT.Exp, scale=-0.5).then_inc(rn_sem, 1)

            def rstd_main(C):
                for g in range(2):
                    act.wait_ge(ss_pe, 2 * C + g + 1)
                    rstd(C, g, ps[:, 2 + g, :].rearrange("p (n t) -> p n t", n=4), 2 * C + g + 1,
                         ln_act, rn_act, SC)

            def copy_o(C):
                c = C % NSC
                for g in range(2):
                    act.wait_ge(o_pe, 2 * C + g + 1)
                    o = ps[:, 6 + g, :].rearrange("p (n t) -> p n t", n=4)
                    nc.scalar.activation(p_main[:, c, 4 * g:4 * g + 4, :], o, ACT.Copy).then_inc(o_act, 1)
                    nc.scalar.activation(sum_place(C, g), o, ACT.Square).then_inc(osq_act, 1)

            act.wait_ge(lb_v, 1)
            nc.scalar.activation(lbw[:, 0:2, :], lbw[:, 0:2, :], ACT.Exp).then_inc(lb_e, 1)
            act.sem_inc(ev_a, 2)
            for h in range(2):
                u0 = HALF_UNITS * h
                if h == 0:
                    split_hi(0)
                norm(h)
                bc = (h == 0)
                with act.Fori(0, A_UNITS // 2) as i:
                    for e in range(2):
                        u = u0 + e
                        s = slot_of(u + 1)
                        act.wait_ge(raw0_ld, i * 32 + 16 * (u + 2))
                        nc.scalar.activation(whi[s][:], raw0[:], ACT.Copy).then_inc(hi_done, 1)
                        act.wait_ge(used, i * 2 + (u + 1))
                        b0 = 4 * (u % 2)
                        tile = i * 4 + 2 * e
                        for q in range(2):
                            src = ps[:, b0 + q, 0:256].rearrange("p (c o t) -> p c o t", c=2, o=1)
                            last = nc.scalar.activation(p_main[:, 2 * q:2 * q + 2, bass.ds(tile, 1), :], src, ACT.Copy)
                        if h == 0:
                            src = ps[:, b0 + 1, 256:256 + NS].unsqueeze(1)
                            last = nc.scalar.activation(p_samp[:, bass.ds(tile, 1), :], src, ACT.Copy)
                        last.then_inc(ev_a, 1)
                u = u0 + L_UNIT
                split_hi(u + 1)
                act.wait_ge(used, u + 1)
                nc.scalar.activation(lr_t[h][:, 0:256], ps[0:RANK, 4 * (u % 2), 0:256], ACT.Copy).then_inc(ev_a, 1)

                def values(v):
                    u = u0 + V0_UNIT + v
                    split_hi(u + 1)
                    act.wait_ge(used, u + 1)
                    for t in range(2):
                        last = nc.scalar.activation(val[:, t, 256 * v:256 * (v + 1)],
                                                    ps[:, 4 * (u % 2), 256 * t:256 * (t + 1)], ACT.Copy)
                    last.then_inc(ev_a, 1)

                values(0)
                act.wait_ge(ev_v, u0 + L_UNIT + 3)
                act.wait_ge(ev_a, 2 + act_copies_before(u0 + V0_UNIT + 1))
                parts = [p_main[:, :, a:b, :] for a, b in ((2, 6), (GT, A_TILES))]
                parts += [p_samp[:, a:b, :] for a, b in ((2, 6), (GT, A_TILES))] if bc else []
                for part in parts:
                    nc.scalar.activation(part, part, ACT.Silu).then_inc(silu_done, 1)
                parts = [p_main[:, :, FT:FT + HB, :]] + ([p_samp[:, FT:FT + HB, :]] if bc else [])
                for part in parts:
                    nc.scalar.activation(part, part, ACT.Sigmoid).then_inc(sig_done, 1)
                parts = [p_main[:, :, 0:2, :]] + ([p_samp[:, 0:2, :]] if bc else [])
                for part in parts:
                    last = nc.scalar.mul(part, part, KA ** -0.5)
                last.then_inc(qs_done, 1)
                values(1)
                act.preload_act_table_set("natural_log_exp_and_others")
                act.wait_ge(f_done, h + 1)
                nc.scalar.activation(b_main[:, :, 2:6, :], p_main[:, :, FT:FT + HB, :], ACT.Ln).then_inc(lnf_done, 1)
                if bc:
                    nc.scalar.activation(b_samp[:, 2:6, :], p_samp[:, FT:FT + HB, :], ACT.Ln).then_inc(lnf_done, 1)
                values(2)
                act.wait_ge(z_dve, h + 1)
                if bc:
                    act.wait_ge(z_s_dve, 1)
                azs = [(az_m, b_main[:, :, 0:2, :])] + ([(az_s, b_samp[:, 0:2, :])] if bc else [])
                base = 0 if h == 0 else 2
                for n, (az, z) in enumerate(azs):
                    nc.scalar.activation(az, z, ACT.Abs).then_inc(az_done, 1)
                    act.wait_ge(az_done, base + n + 1)
                    nc.scalar.activation(az, az, ACT.Exp, scale=-1.0).then_inc(aze_done, 1)
                    act.wait_ge(aze_done, base + n + 1)
                    nc.scalar.activation(az, az, ACT.Ln, bias=ones[:, 0:1]).then_inc(azl_done, 1)
                values(3)

                C0 = NSC * h
                exps(C0)
                exp_d(C0)
                for c in range(NSC):
                    C = C0 + c
                    if c + 1 < NSC:
                        exps(C + 1)
                    act.wait_ge(kt_pe, C + 1)
                    if C >= 1:
                        act.wait_ge(kv_pe, C)
                    if c == 0:
                        act.wait_ge(used, u0 + O0_UNIT)
                    nc.scalar.activation(kT_st[:, 0:4, :], ps[:, 2, :].rearrange("p (s t) -> p s t", s=4), ACT.Copy)
                    nc.scalar.activation(kT_st[:, 4:6, :], ps[:, 3, 0:256].rearrange("p (s t) -> p s t", s=2),
                                         ACT.Copy).then_inc(kt_act, 1)
                    if c + 1 < NSC:
                        exp_d(C + 1)
                    if c >= 1:
                        rstd_main(C - 1)
                    copy_o(C)
                if h == 0:
                    act.wait_ge(s_b, 1)
                    act.wait_ge(o_pe, 2 * 3)
                    act.wait_ge(pool_q, 3)
                    act.wait_ge(pool_k, 3)
                    bs = b_samp[:].rearrange("p s (b t) -> p s b t", b=SB)[:, :, :, ST - 1:ST]
                    nc.scalar.activation(sq_in[:], b_samp[:], ACT.Exp).then_inc(s_e1, 1)
                    nc.scalar.activation(sk_in[:], b_samp[:], ACT.Exp, scale=-1.0).then_inc(s_e1, 1)
                    nc.scalar.activation(dsamp.unsqueeze(3), bs, ACT.Exp).then_inc(s_e1, 1)
                    act.wait_ge(s_d, 1)
                    nc.scalar.activation(sk_out[:], sk_out[:], ACT.Exp).then_inc(s_e3, 1)
                rstd_main(C0 + NSC - 1)
                if h == 0:
                    act.wait_ge(s_o, 1)
                    for g in range(2):
                        so = ps[:, g, 0:4 * NS].rearrange("p (n t) -> p n t", n=4)
                        nc.scalar.activation(p_samp[:, 4 * g:4 * g + 4, :], so, ACT.Copy).then_inc(s_ocp, 1)
                        nc.scalar.activation(sum_place(0, g, True), so, ACT.Square).then_inc(s_osq, 1)
                    act.wait_ge(s_ss, 1)
                    for g in range(2):
                        rstd(0, g, ps[:, g, 4 * NS:8 * NS].rearrange("p (n t) -> p n t", n=4), g + 1,
                             s_ln, s_rn, NS, True)

                act.wait_ge(o_pe, 2 * NSC * (h + 1))
                act.wait_ge(og_pool, NSC * (h + 1))
                if h == 0:
                    act.wait_ge(s_kv, SLOTS)
                    act.wait_ge(s_og, 1)
                for n in range(NH):
                    last = nc.scalar.activation(h_hi[:, n, 0:HALF].rearrange("p (c t) -> p c t", c=NSC),
                                                p_main[:, :, n, :], ACT.Copy)
                    if bc:
                        last = nc.scalar.activation(h_hi[:, n, HALF:HALF + NS], p_samp[:, n, :], ACT.Copy)
                    last.then_inc(oh_act, 1)
                for r in range(O0_UNIT, HALF_UNITS):
                    split_hi(u0 + r + 1)

            norm(2)
            norm(3)
            norm(4)
            act.wait_ge(raw1_ld, 16)
            nc.scalar.activation(whi[1][:], raw1[:], ACT.Copy).then_inc(hi_done, 1)

            def ffn_group(i, last_group):
                def split_w2():
                    act.wait_ge(raw0_ld, i * 32 + 16 * (F0_UNIT + 2))
                    nc.scalar.activation(whi[2][:], raw0[:], ACT.Copy).then_inc(hi_done, 1)

                for st in range(6):
                    act.wait_ge(step_pe, i * 6 + (st + 1))
                    act.wait_ge(gl_done, i * 6 + (st + 1))
                    ch, ft = divmod(st, 2)
                    w = FF_CHUNKS[ch][1]
                    nc.scalar.activation(gated[:, st % 2, 0:w], ps[:, 2 * (st % 2), 0:w], ACT.Silu).then_inc(silu_f, 1)
                    if st == 1:
                        split_w2()
                if not last_group:
                    act.wait_ge(raw0_ld, i * 32 + 16 * (F0_UNIT + 3))
                    nc.scalar.activation(whi[0][:], raw0[:], ACT.Copy).then_inc(hi_done, 1)
                    act.wait_ge(raw1_ld, i * 16 + 32)
                    nc.scalar.activation(whi[1][:], raw1[:], ACT.Copy).then_inc(hi_done, 1)

            with act.Fori(0, GROUPS - 1) as i:
                ffn_group(i, False)
            ffn_group(GROUPS - 1, True)
            for t in range(9):
                rows = P if t < 8 else NS
                act.wait_ge(y_dve, (GROUPS - 1) * 18 + 2 * (t + 1) + 4)
                if t >= 1:
                    act.wait_ge(sqf, t)
                nc.scalar.activation(raw1[0:rows, 0:D], x_res[0:rows, PLACE[t], :], ACT.Square,
                                     accum_out=ms[0:rows, t:t + 1]).then_inc(sqf, 1)
                act.wait_ge(sqf, t + 1)
                nc.scalar.activation(ms[0:rows, t:t + 1], ms[0:rows, t:t + 1], ACT.Sqrt, scale=1.0 / D,
                                     bias=eps_t[0:rows]).then_inc(rmsf, 1)

        @block.vector
        def _(dve):
            def split_lo(u):
                size = 1024 if u % HALF_UNITS == L_UNIT else 2048
                dve.wait_ge(hi_done, u + 1)
                s = slot_of(u)
                nc.vector.tensor_tensor(wlo[s][:, 0:size], raw0[:, 0:size], whi[s][:, 0:size].bitcast(F32),
                                        ALU.subtract).then_inc(lo_done, 1)

            def norm(n):
                main, samp, hi, lo, mcol, scol, gain = stage_parts(n)
                g0, cnt = groups_before(n), tiles_before(n)
                for m, (place, num, rows) in enumerate(row_groups(n)):
                    dve.wait_ge(rms_done, g0 + m + 1)
                    nc.vector.reciprocal(rs[0:rows, place:place + num],
                                         ms[0:rows, place:place + num]).then_inc(rs_done, 1)
                dve.wait_ge(rs_done, groups_before(n + 1))
                for place, rows, scratch in main + ([samp] if samp else []):
                    nc.vector.tensor_scalar(scratch, x_res[0:rows, place, :], rs[0:rows, place:place + 1], None,
                                            ALU.mult).then_inc(xn_done, 1)
                t0 = turns_before(n)

                def part(width, src, k, col):
                    return nc.vector.scalar_tensor_tensor(
                        out=lo[:, k, col:col + width], in0=src, scalar=pv[:, gain + k:gain + k + 1],
                        in1=hi[:, k, col:col + width].bitcast(F32), op0=ALU.mult, op1=ALU.subtract)

                if main:
                    for k in range(KT_D):
                        dve.wait_ge(th_done, t0 + k + 1)
                        part(HALF, ps[:, k % 4, :], k, mcol).then_inc(tl_done, 1)
                if samp:
                    dve.wait_ge(th_done, turns_before(n + 1))
                    for k in range(KT_D):
                        last = part(NS, ps[:, 4, k * NS:(k + 1) * NS], k, scol)
                    last.then_inc(tl_done, 1)

            def d_of(C):
                c, j = C % NSC, C % 2
                dve.wait_ge(used, HALF_UNITS * (C // NSC) + O0_UNIT)
                dve.wait_ge(b_done, C + 1)
                if C >= 2:
                    dve.wait_ge(att_pe, 2 * (C - 1))
                    dve.wait_ge(pool_k, C - 1)
                b = b_main[:, c].rearrange("p s (c t) -> p (s c) t", t=CH)
                nc.vector.tensor_tensor(k_out[j][:].rearrange("p s (c t) -> p (s c) t", t=CH),
                                        b[:, :, CH - 1:CH].broadcast_to((P, SLOTS * NCH, CH)), b,
                                        ALU.subtract).then_inc(d_done, 1)

            def prep(C):
                c, j = C % NSC, C % 2
                q, k = p_main[:, c, QT:QT + SLOTS, :], p_main[:, c, KTL:KTL + SLOTS, :]
                dve.wait_ge(e1_done, 3 * (C + 1))
                nc.vector.tensor_tensor(q_in[j][:], q_in[j][:], q, ALU.mult)
                nc.vector.tensor_tensor(k_in[j][:], k_in[j][:], k, ALU.mult)
                dve.wait_ge(e3_done, C + 1)
                nc.vector.tensor_tensor(k_out[j][:], k_out[j][:], k, ALU.mult).then_inc(prep1_done, 1)
                dve.wait_ge(prep1_done, C + 1)
                dve.wait_ge(fac_a, C + 1)

                def chunks(buf, first):
                    return buf[:, :, first:first + 64].rearrange("p s (c t) -> p s c t", c=2)

                nc.vector.tensor_tensor(chunks(q_64[j], 0), chunks(q_in[j], 64),
                                        f64[j].unsqueeze(3).broadcast_to((P, SLOTS, 2, CH)), ALU.mult)
                nc.vector.tensor_tensor(chunks(k_64[j], 0), chunks(k_out[j], 0),
                                        g64[j].unsqueeze(3).broadcast_to((P, SLOTS, 2, CH)),
                                        ALU.mult).then_inc(prep_done, 1)

            def mask(C):
                for g in range(2):
                    dve.wait_ge(att_pe, 2 * C + g + 1)
                    dve.wait_ge(zero_att, C // NSC + 1)
                    if C >= 1:
                        dve.wait_ge(o_pe, 2 * (C - 1) + g + 1)
                    nc.vector.copy_predicated(att[:, g], causal.unsqueeze(1).broadcast_to((P, 4, SC)),
                                              ps[:, g, :].rearrange("p (n t) -> p n t", n=4)).then_inc(att_dve, 1)

            def norm_o(C):
                c = C % NSC
                for g in range(2):
                    dve.wait_ge(rn_act, 2 * C + g + 1)
                    o = p_main[:, c, 4 * g:4 * g + 4, :]
                    nc.vector.tensor_tensor(o, o, sum_place(C, g), ALU.mult).then_inc(on_dve, 1)

            def update_state(C):
                j = C % 2
                dve.wait_ge(kv_pe, C + 1)
                dve.wait_ge(o_pe, 2 * (C + 1))
                dve.wait_ge(fac_b, C + 1)
                if C == 0:
                    dve.wait_ge(zero_state, 1)
                else:
                    dve.wait_ge(st_done, C)
                for slot in range(SLOTS):
                    bank, at = (4, slot) if slot < 4 else (5, slot - 4)
                    last = nc.vector.scalar_tensor_tensor(
                        out=state[:, slot, :], in0=state[:, slot, :], scalar=dtot[j][:, slot, :],
                        in1=ps[:, bank, at * V:(at + 1) * V], op0=ALU.mult, op1=ALU.add)
                last.then_inc(st_done, 1)

            nc.vector.memset(val[NS:P, 4, :], 0.0)
            dve.wait_ge(c_ld, 48)
            lbp = pv[:, V_LB:V_LB + 8].rearrange("p (a n) -> p a n", a=2)
            nc.vector.tensor_tensor(lbw[:, 2, :], lbp[:, 0, :], lbp[:, 1, :], ALU.max).then_inc(zm_done, 1)
            dve.wait_ge(zm_done, 1)
            nc.vector.tensor_tensor(lbw[:, 0:2, :], lbp, lbw[:, 2:3, :].broadcast_to((P, 2, HB)),
                                    ALU.subtract).then_inc(lb_v, 1)
            dve.wait_ge(lb_e, 1)
            nc.vector.tensor_tensor(lbw[:, 2, :], lbw[:, 0, :], lbw[:, 1, :], ALU.add).then_inc(lb_v, 1)
            dve.wait_ge(lb_v, 2)
            nc.vector.reciprocal(lbw[:, 2, :], lbw[:, 2, :]).then_inc(lb_v, 1)
            dve.wait_ge(lb_v, 3)
            nc.vector.tensor_tensor(lb, lbw[:, 0, :], lbw[:, 2, :], ALU.mult).then_inc(lb_v, 1)
            dve.wait_ge(lb_v, 4)
            nc.vector.tensor_scalar(omlb, lb, -1.0, 1.0, ALU.mult, ALU.add).then_inc(lb_v, 1)
            dve.wait_ge(lb_v, 5)

            dve.sem_inc(ev_v, 2)
            for h in range(2):
                u0 = HALF_UNITS * h
                bc = (h == 0)
                if h == 0:
                    split_lo(0)
                norm(h)
                with dve.Fori(0, A_UNITS // 2) as i:
                    for e in range(2):
                        u = u0 + e
                        s = slot_of(u + 1)
                        dve.wait_ge(hi_done, i * 2 + (u + 2))
                        nc.vector.tensor_tensor(wlo[s][:], raw0[:], whi[s][:].bitcast(F32),
                                                ALU.subtract).then_inc(lo_done, 1)
                        dve.wait_ge(used, i * 2 + (u + 1))
                        b0 = 4 * (u % 2) + 2
                        tile = i * 4 + (2 * e + 1)
                        for q in range(2):
                            src = ps[:, b0 + q, 0:256].rearrange("p (c o t) -> p c o t", c=2, o=1)
                            last = nc.vector.tensor_copy(p_main[:, 2 * q:2 * q + 2, bass.ds(tile, 1), :], src)
                        if bc:
                            last = nc.vector.tensor_copy(p_samp[:, bass.ds(tile, 1), :],
                                                         ps[:, b0 + 1, 256:256 + NS].unsqueeze(1))
                        last.then_inc(ev_v, 1)
                u = u0 + L_UNIT
                split_lo(u + 1)
                dve.wait_ge(used, u + 1)
                w = 256 + half(h)
                nc.vector.tensor_copy(lr_t[h][:, 256:256 + w], ps[0:RANK, 4 * (u % 2) + 1, 0:w]).then_inc(ev_v, 1)

                def values(v):
                    u = u0 + V0_UNIT + v
                    split_lo(u + 1)
                    dve.wait_ge(used, u + 1)
                    for t in range(2, 5 if bc else 4):
                        rows = P if t < 4 else NS
                        last = nc.vector.tensor_copy(
                            val[0:rows, t, 256 * v:256 * (v + 1)],
                            ps[0:rows, 4 * (u % 2) + t // 2, 256 * (t % 2):256 * (t % 2 + 1)])
                    last.then_inc(ev_v, 1)

                values(0)
                for p in range(2):
                    dve.wait_ge(z_pe, 2 * h + p + 1)
                    last = nc.vector.tensor_scalar(
                        b_main[:, :, p, :], ps[:, 3 + 4 * p, :].rearrange("p (c t) -> p c t", c=NSC),
                        pv[:, V_BA + p:V_BA + p + 1], None, ALU.add)
                last.then_inc(z_dve, 1)
                dve.wait_ge(sig_done, 2 if h == 0 else 3)
                for n in range(HB):
                    fs = [p_main[:, :, FT + n, :]] + ([p_samp[:, FT + n, :]] if bc else [])
                    for f in fs:
                        last = nc.vector.tensor_scalar(f, f, omlb[:, n:n + 1], lb[:, n:n + 1], ALU.mult, ALU.add)
                last.then_inc(f_done, 1)
                values(1)
                if bc:
                    dve.wait_ge(z_s_pe, 1)
                    for p in range(2):
                        last = nc.vector.tensor_scalar(b_samp[:, p, :], ps[:, 3, p * NS:(p + 1) * NS],
                                                       pv[:, V_BA + p:V_BA + p + 1], None, ALU.add)
                    last.then_inc(z_s_dve, 1)
                dve.wait_ge(silu_done, 4 if h == 0 else 6)
                for a, col in ((GT, V_ONA), (GT + 2, V_ONB), (GT + 4, V_ONA), (GT + 6, V_ONB)):
                    gs = [p_main[:, :, a:a + 2, :]] + ([p_samp[:, a:a + 2, :]] if bc else [])
                    for g in gs:
                        last = nc.vector.tensor_scalar(g, g, pv[:, col:col + 1], None, ALU.mult)
                last.then_inc(g_done, 1)
                values(2)
                dve.wait_ge(lnf_done, 2 if h == 0 else 3)
                ks = [p_main[:, :, FT:FT + HB, :]] + ([p_samp[:, FT:FT + HB, :]] if bc else [])
                for k in ks:
                    last = nc.vector.tensor_scalar(k, k, -1.0, 1.0, ALU.mult, ALU.add)
                last.then_inc(k_done, 1)
                dve.wait_ge(azl_done, 2 if h == 0 else 3)
                zs = [(b_main[:, :, 0:2, :], az_m)] + ([(b_samp[:, 0:2, :], az_s)] if bc else [])
                for z, l in zs:
                    last = nc.vector.scalar_tensor_tensor(out=z, in0=z, scalar=0.0, in1=l, op0=ALU.min,
                                                          op1=ALU.subtract)
                last.then_inc(la_done, 1)
                dve.wait_ge(la_done, h + 1)
                for z, _ in zs:
                    last = nc.vector.tensor_scalar(z, z, 1.0 / GATE_NORM, None, ALU.mult)
                last.then_inc(la2_done, 1)
                dve.wait_ge(la2_done, h + 1)
                for c in range(NSC):
                    b = b_main[:, c].rearrange("p s t -> p (s t)")
                    nc.vector.tensor_tensor_scan(b, m32, b, 0.0, ALU.mult, ALU.add).then_inc(b_done, 1)
                if bc:
                    b = b_samp[:].rearrange("p s t -> p (s t)")
                    nc.vector.tensor_tensor_scan(b, m8, b, 0.0, ALU.mult, ALU.add).then_inc(s_b, 1)
                values(3)

                dve.wait_ge(qs_done, h + 1)
                dve.wait_ge(k_done, h + 1)
                dve.wait_ge(g_done, h + 1)
                C0 = NSC * h
                d_of(C0)
                prep(C0)
                for c in range(NSC):
                    C = C0 + c
                    if c + 1 < NSC:
                        d_of(C + 1)
                    mask(C)
                    if c + 1 < NSC:
                        prep(C + 1)
                    if c >= 1:
                        norm_o(C - 1)
                    update_state(C)
                if h == 0:
                    dve.wait_ge(s_b, 1)
                    dve.wait_ge(att_pe, 2 * 3)
                    dve.wait_ge(o_pe, 2 * 3)
                    dve.wait_ge(pool_k, 3)
                    b = b_samp[:].rearrange("p s (b t) -> p (s b) t", t=ST)
                    nc.vector.tensor_tensor(sk_out[:].rearrange("p s (b t) -> p (s b) t", t=ST),
                                            b[:, :, ST - 1:ST].broadcast_to((P, SLOTS * SB, ST)), b,
                                            ALU.subtract).then_inc(s_d, 1)
                    dve.wait_ge(s_e1, 3)
                    nc.vector.tensor_tensor(sq_in[:], sq_in[:], p_samp[:, QT:QT + SLOTS, :], ALU.mult)
                    nc.vector.tensor_tensor(sk_in[:], sk_in[:], p_samp[:, KTL:KTL + SLOTS, :], ALU.mult)
                    dve.wait_ge(s_e3, 1)
                    nc.vector.tensor_tensor(sk_out[:], sk_out[:], p_samp[:, KTL:KTL + SLOTS, :],
                                            ALU.mult).then_inc(s_prep, 1)
                    dve.wait_ge(s_att_pe, 1)
                    dve.wait_ge(s_zero, 1)
                    for g in range(2):
                        last = nc.vector.copy_predicated(
                            s_att[0:NS, 4 * g:4 * g + 4, :], smask.unsqueeze(1).broadcast_to((NS, 4, NS)),
                            ps[0:NS, g, 0:4 * NS].rearrange("p (n t) -> p n t", n=4))
                    last.then_inc(s_att_dve, 1)
                norm_o(C0 + NSC - 1)
                if h == 0:
                    def mask_kT(slot):
                        dve.wait_ge(s_t, 1)
                        if slot >= 2:
                            dve.wait_ge(s_kv, slot - 1)
                        bank, at = (4, slot) if slot < 4 else (5, slot - 4)
                        nc.vector.tensor_tensor(
                            skT[slot % 2][:], ps[0:NS, bank, at * P:(at + 1) * P].unsqueeze(1).broadcast_to((NS, SB, P)),
                            bmask.unsqueeze(2).broadcast_to((NS, SB, P)), ALU.mult).then_inc(s_dm, 1)

                    mask_kT(0)
                    mask_kT(1)
                    dve.wait_ge(s_rn, 2)
                    for g in range(2):
                        o = p_samp[:, 4 * g:4 * g + 4, :]
                        last = nc.vector.tensor_tensor(o, o, sum_place(0, g, True), ALU.mult)
                    last.then_inc(s_on, 1)
                    for slot in range(SLOTS):
                        dve.wait_ge(s_kv, slot + 1)
                        dve.wait_ge(s_decayed, slot + 1)
                        b0 = 6 if slot % 2 == 0 else 2
                        st = s_state[:, :, slot, :]
                        for q in range(2):
                            last = nc.vector.tensor_tensor(st[:, 4 * q:4 * q + 4, :], st[:, 4 * q:4 * q + 4, :],
                                                           ps[:, b0 + q, :].rearrange("p (b v) -> p b v", b=4), ALU.add)
                        last.then_inc(s_upd, 1)
                        if slot + 2 < SLOTS:
                            mask_kT(slot + 2)

                for n in range(NH):
                    dve.wait_ge(oh_act, NH * h + n + 1)
                    last = nc.vector.tensor_tensor(h_lo[:, n, 0:HALF].rearrange("p (c t) -> p c t", c=NSC),
                                                   p_main[:, :, n, :],
                                                   h_hi[:, n, 0:HALF].rearrange("p (c t) -> p c t", c=NSC).bitcast(F32),
                                                   ALU.subtract)
                    if bc:
                        last = nc.vector.tensor_tensor(h_lo[:, n, HALF:HALF + NS], p_samp[:, n, :],
                                                       h_hi[:, n, HALF:HALF + NS].bitcast(F32), ALU.subtract)
                    last.then_inc(ol_dve, 1)
                if h == 0:
                    dve.wait_ge(xr_ld, 64)
                for r in range(O0_UNIT, HALF_UNITS):
                    u = u0 + r
                    split_lo(u + 1)
                    dve.wait_ge(used, u + 1)
                    cols = slice(256 * (r - O0_UNIT), 256 * (r - O0_UNIT + 1))
                    for t, (place, rows, _) in enumerate(half_tiles(h)):
                        x = x_res[0:rows, place, cols]
                        last = nc.vector.tensor_tensor(
                            x, ps[0:rows, 4 * (u % 2) + t // 2, 256 * (t % 2):256 * (t % 2 + 1)], x, ALU.add)
                    last.then_inc(ev_v, 1)

            norm(2)
            norm(3)
            norm(4)

            def lo_of(slot, raw, count):
                dve.wait_ge(hi_done, count)
                nc.vector.tensor_tensor(wlo[slot][:], raw[:], whi[slot][:].bitcast(F32),
                                        ALU.subtract).then_inc(lo_done, 1)

            lo_of(1, raw1, F0_UNIT + 2)
            dve.sem_inc(gl_done, 2)
            dve.sem_inc(y_dve, 4)

            def ffn_group(i, last_group):
                for st in range(6):
                    ch, ft = divmod(st, 2)
                    col, w = FF_CHUNKS[ch]
                    n, s = i * 6 + (st + 1), st % 2
                    dve.wait_ge(silu_f, n)
                    nc.vector.tensor_tensor(gated[:, s, 0:w], gated[:, s, 0:w], ps[:, 2 * s + 1, 0:w],
                                            ALU.mult).then_inc(gm_done, 1)
                    dve.wait_ge(gm_done, n)
                    hi = g_hi[:, ft, col:col + w]
                    nc.vector.tensor_copy(hi, gated[:, s, 0:w]).then_inc(gh_done, 1)
                    dve.wait_ge(gh_done, n)
                    nc.vector.tensor_tensor(g_lo[:, ft, col:col + w], gated[:, s, 0:w], hi.bitcast(F32),
                                            ALU.subtract).then_inc(gl_done, 1)
                    if st == 1:
                        lo_of(2, raw0, i * 3 + (F0_UNIT + 3))
                for t in range(9):
                    rows = P if t < 8 else NS
                    for q in range(2):
                        m = 2 * t + q
                        dve.wait_ge(y_pe, i * 18 + (m + 1))
                        x = x_res[0:rows, PLACE[t], 512 * q:512 * (q + 1)]
                        nc.vector.tensor_tensor(x, ps[0:rows, 4 + m % 4, :], x, ALU.add).then_inc(y_dve, 1)
                    if not last_group and t == 2:
                        lo_of(0, raw0, i * 3 + (F0_UNIT + 4))
                    if not last_group and t == 5:
                        lo_of(1, raw1, i * 3 + (F0_UNIT + 5))

            with dve.Fori(0, GROUPS - 1) as i:
                ffn_group(i, False)
            ffn_group(GROUPS - 1, True)
            dve.wait_ge(nf_ld, 16)
            for t in range(9):
                rows = P if t < 8 else NS
                dve.wait_ge(rmsf, t + 1)
                nc.vector.reciprocal(rs[0:rows, t:t + 1], ms[0:rows, t:t + 1]).then_inc(rsf, 1)
                dve.wait_ge(rsf, t + 1)
                x = x_res[0:rows, PLACE[t], :]
                nc.vector.scalar_tensor_tensor(out=x, in0=x, scalar=rs[0:rows, t:t + 1], in1=nf[0:rows, :],
                                               op0=ALU.mult, op1=ALU.mult).then_inc(yf_done, 1)

        @block.tensor
        def _(pe):
            def three(out, a_hi, a_lo, b_hi, b_lo, first, last):
                nc.tensor.matmul(out, a_hi, b_hi, start=first, stop=False)
                nc.tensor.matmul(out, a_hi, b_lo, start=False, stop=False)
                return nc.tensor.matmul(out, a_lo, b_hi, start=False, stop=last)

            def norm(n):
                main, samp, hi, lo, mcol, scol, gain = stage_parts(n)
                t0, cnt = turns_before(n), tiles_before(n)
                if n == 1:
                    pe.wait_ge(ev_v, HALF_UNITS + 2)
                if n == 2:
                    pe.wait_ge(ev_v, F0_UNIT + 2)
                if main:
                    pe.wait_ge(xn_done, cnt + 4)
                    for k in range(KT_D):
                        if k >= 4:
                            pe.wait_ge(tl_done, t0 + k - 3)
                        elif n >= 1:
                            pe.wait_ge(tl_done, t0)
                        for j, (_, _, scratch) in enumerate(main):
                            last = nc.tensor.transpose(ps[:, k % 4, j * P:(j + 1) * P],
                                                       scratch[:, k * P:(k + 1) * P], ident)
                        last.then_inc(tr_done, 1)
                if samp:
                    pe.wait_ge(xn_done, tiles_before(n + 1))
                    for k in range(KT_D):
                        last = nc.tensor.transpose(ps[:, 4, k * NS:(k + 1) * NS],
                                                   samp[2][:, k * P:(k + 1) * P], ident[0:NS, 0:NS])
                    last.then_inc(tr_done, 1)

            pe.wait_ge(c_ld, 48)
            for h in range(2):
                u0 = HALF_UNITS * h
                chunks = [(0, 256), (256, 256 + half(h))]
                norm(h)
                pe.wait_ge(tl_done, turns_before(h + 1))
                with pe.Fori(0, A_UNITS // 2) as i:
                    for e in range(2):
                        u = u0 + e
                        s = slot_of(u)
                        pe.wait_ge(lo_done, i * 2 + (u + 1))
                        pe.wait_ge(ev_v, i * 2 + (u + 1))
                        pe.wait_ge(ev_a, i * 2 + (O0_UNIT * h + e + 1))
                        w_hi = whi[s][:].rearrange("p (k n) -> p k n", k=KT_D)
                        w_lo = wlo[s][:].rearrange("p (k n) -> p k n", k=KT_D)
                        for ft in range(2):
                            for q, (col, w) in enumerate(chunks):
                                for k in range(KT_D):
                                    a, b = slice(ft * P, (ft + 1) * P), slice(col, col + w)
                                    last = three(ps[:, 4 * (u % 2) + 2 * ft + q, 0:w],
                                                 w_hi[:, k, a], w_lo[:, k, a], h_hi[:, k, b], h_lo[:, k, b],
                                                 k == 0, k == KT_D - 1)
                        last.then_inc(used, 1)
                u = u0 + L_UNIT
                s = slot_of(u)
                pe.wait_ge(lo_done, u + 1)
                pe.wait_ge(ev_v, u + 1)
                pe.wait_ge(ev_a, 2 + act_copies_before(u - 1))
                w_hi = whi[s][:, 0:1024].rearrange("p (k n) -> p k n", k=KT_D)
                w_lo = wlo[s][:, 0:1024].rearrange("p (k n) -> p k n", k=KT_D)
                for q, (col, w) in enumerate(chunks):
                    for k in range(KT_D):
                        b = slice(col, col + w)
                        last = three(ps[:, 4 * (u % 2) + q, 0:w], w_hi[:, k], w_lo[:, k],
                                     h_hi[:, k, b], h_lo[:, k, b], k == 0, k == KT_D - 1)
                last.then_inc(used, 1)

                def token_major(r):
                    u = u0 + r
                    s = slot_of(u)
                    pe.wait_ge(lo_done, u + 1)
                    pe.wait_ge(ev_v, u + 1)
                    pe.wait_ge(ev_a, 2 + act_copies_before(u - 1))
                    w_hi = whi[s][:].rearrange("p (k n) -> p k n", k=KT_D)
                    w_lo = wlo[s][:].rearrange("p (k n) -> p k n", k=KT_D)
                    for t, (_, rows, col) in enumerate(half_tiles(h)):
                        for k in range(KT_D):
                            a = slice(col, col + rows)
                            last = three(ps[0:rows, 4 * (u % 2) + t // 2, 256 * (t % 2):256 * (t % 2 + 1)],
                                         h_hi[:, k, a], h_lo[:, k, a], w_hi[:, k], w_lo[:, k],
                                         k == 0, k == KT_D - 1)
                    last.then_inc(used, 1)

                token_major(V0_UNIT)
                pe.wait_ge(ev_a, 2 + act_copies_before(u0 + V0_UNIT))
                pe.wait_ge(ev_v, u0 + V0_UNIT + 2)
                for p in range(2):
                    nc.tensor.matmul(ps[:, 3 + 4 * p, :], wa2[:, p * P:(p + 1) * P], lr_t[h][:, 0:HALF],
                                     start=True, stop=True).then_inc(z_pe, 1)
                token_major(V0_UNIT + 1)
                if h == 0:
                    pe.wait_ge(z_dve, 1)
                    for p in range(2):
                        last = nc.tensor.matmul(ps[:, 3, p * NS:(p + 1) * NS], wa2[:, p * P:(p + 1) * P],
                                                lr_t[0][:, HALF:HALF + NS], start=True, stop=True)
                    last.then_inc(z_s_pe, 1)
                token_major(V0_UNIT + 2)
                token_major(V0_UNIT + 3)

                pe.wait_ge(ev_a, 2 + act_copies_before(u0 + O0_UNIT))
                pe.wait_ge(ev_v, u0 + O0_UNIT + 2)

                def sums(C):
                    for g in range(2):
                        pe.wait_ge(osq_act, 2 * C + g + 1)
                        nc.tensor.matmul(ps[:, 2 + g, :].rearrange("p (n t) -> p n t", n=4), ones,
                                         sum_place(C, g), start=True, stop=True).then_inc(ss_pe, 1)

                C0 = NSC * h
                for c in range(NSC):
                    C = C0 + c
                    j = C % 2
                    pe.wait_ge(pool_k, C + 1)
                    if C >= 2:
                        pe.wait_ge(ln_act, 2 * (C - 1) if c else 2 * C)
                    for slot in range(SLOTS):
                        bank, at = (2, slot) if slot < 4 else (3, slot - 4)
                        last = nc.tensor.transpose(ps[:, bank, at * P:(at + 1) * P], k_st[:, slot, :], ident)
                    last.then_inc(kt_pe, 1)
                    pe.wait_ge(prep_done, C + 1)
                    for g in range(2):
                        if C >= 1:
                            pe.wait_ge(att_dve, 2 * (C - 1) + g + 1)
                        for at, n in enumerate(ORDER[4 * g:4 * g + 4]):
                            slot, lo, kw = head_place(n)
                            r, o = slice(lo, lo + kw), at * SC
                            nc.tensor.matmul(ps[:, g, o:o + SC], k_in[j][r, slot, :], q_in[j][r, slot, :],
                                             start=True, stop=True)
                            for a in (0, 64):
                                nc.tensor.matmul(ps[a:a + 32, g, o + a + 32:o + a + 64], k_out[j][r, slot, a:a + 32],
                                                 q_in[j][r, slot, a + 32:a + 64], start=True, stop=True)
                            last = nc.tensor.matmul(ps[0:64, g, o + 64:o + SC], k_64[j][r, slot, :],
                                                    q_64[j][r, slot, :], start=True, stop=True)
                        last.then_inc(att_pe, 1)
                    pe.wait_ge(kt_act, C + 1)
                    if C >= 1:
                        pe.wait_ge(st_done, C)
                    for n in range(NH):
                        slot, lo, kw = head_place(n)
                        bank, at = (4, slot) if slot < 4 else (5, slot - 4)
                        last = nc.tensor.matmul(ps[lo:lo + kw, bank, at * V:(at + 1) * V], kT_st[:, slot, lo:lo + kw],
                                                val[:, c, n * V:(n + 1) * V], start=True, stop=True)
                    last.then_inc(kv_pe, 1)
                    if c >= 1:
                        sums(C - 1)
                    pe.wait_ge(pool_q, C + 1)
                    if C == 0:
                        pe.wait_ge(zero_state, 1)
                    for g in range(2):
                        pe.wait_ge(att_dve, 2 * C + g + 1)
                        if C >= 1:
                            pe.wait_ge(osq_act, 2 * (C - 1) + g + 1)
                        for at, n in enumerate(ORDER[4 * g:4 * g + 4]):
                            slot, lo, kw = head_place(n)
                            o = ps[:, 6 + g, at * SC:(at + 1) * SC]
                            nc.tensor.matmul(o, state[lo:lo + kw, slot, :], q_st[j][lo:lo + kw, slot, :],
                                             start=True, stop=False)
                            last = nc.tensor.matmul(o, val[:, c, n * V:(n + 1) * V], att[:, g, at, :],
                                                    start=False, stop=True)
                        last.then_inc(o_pe, 1)
                if h == 0:
                    pe.wait_ge(s_prep, 1)
                    pe.wait_ge(att_dve, 2 * NSC)
                    for m, n in enumerate(ORDER):
                        slot, lo, kw = head_place(n)
                        last = nc.tensor.matmul(ps[0:NS, m // 4, (m % 4) * NS:(m % 4 + 1) * NS], sk_in[lo:lo + kw, slot, :],
                                                sq_in[lo:lo + kw, slot, :], start=True, stop=True)
                    last.then_inc(s_att_pe, 1)
                    pe.wait_ge(st_done, NSC)
                    for slot in range(SLOTS):
                        bank, at = (4, slot) if slot < 4 else (5, slot - 4)
                        last = nc.tensor.transpose(ps[0:NS, bank, at * P:(at + 1) * P], sk_out[:, slot, :], ident)
                    last.then_inc(s_t, 1)
                pe.wait_ge(ln_act, 2 * (C0 + NSC - 1))
                sums(C0 + NSC - 1)
                if h == 0:
                    pe.wait_ge(s_att_dve, 1)
                    pe.wait_ge(st_ld, 16 * NH)
                    for m, n in enumerate(ORDER):
                        slot, lo, kw = head_place(n)
                        g, o = m // 4, (m % 4) * NS
                        nc.tensor.matmul(ps[:, g, o:o + NS], val[:, 4, n * V:(n + 1) * V],
                                         s_att[:, m, :], start=True, stop=False)
                        for b in range(SB):
                            last = nc.tensor.matmul(ps[:, g, o + b * ST:o + (b + 1) * ST],
                                                    s_state[lo:lo + kw, b, slot, :],
                                                    sq_in[lo:lo + kw, slot, b * ST:(b + 1) * ST],
                                                    start=False, stop=(b == SB - 1))
                    last.then_inc(s_o, 1)
                    for slot in range(SLOTS):
                        if slot == 1:
                            pe.wait_ge(s_osq, 2)
                            for g in range(2):
                                last = nc.tensor.matmul(
                                    ps[:, g, 4 * NS:8 * NS].rearrange("p (n t) -> p n t", n=4),
                                    ones, sum_place(0, g, True), start=True, stop=True)
                            last.then_inc(s_ss, 1)
                        pe.wait_ge(s_dm, slot + 1)
                        if slot == 0:
                            pe.wait_ge(osq_act, 2 * NSC)
                        elif slot == 1:
                            pe.wait_ge(ln_act, 2 * NSC)
                        else:
                            pe.wait_ge(s_upd, slot - 1)
                        b0 = 6 if slot % 2 == 0 else 2
                        for n in range(NH):
                            sl, lo, kw = head_place(n)
                            if sl != slot:
                                continue
                            for b in range(SB):
                                last = nc.tensor.matmul(ps[lo:lo + kw, b0 + b // 4, (b % 4) * V:(b % 4 + 1) * V],
                                                        skT[slot % 2][:, b, lo:lo + kw],
                                                        val[0:NS, 4, n * V:(n + 1) * V], start=True, stop=True)
                        last.then_inc(s_kv, 1)
                    pe.wait_ge(s_upd, SLOTS)
                    pe.wait_ge(s_ln, 2)

                pe.wait_ge(osq_act, 2 * NSC * (h + 1))
                pe.wait_ge(ln_act, 2 * NSC * (h + 1))
                pe.wait_ge(st_done, NSC * (h + 1))
                pe.wait_ge(ol_dve, NH * (h + 1))
                for r in range(O0_UNIT, HALF_UNITS):
                    token_major(r)

            norm(2)
            norm(3)
            norm(4)
            pe.wait_ge(tl_done, turns_before(N_STAGES))

            def ffn_group(i):
                w1_hi, w3_hi = (whi[s][:].rearrange("p (k n) -> p k n", k=KT_D) for s in range(2))
                w1_lo, w3_lo = (wlo[s][:].rearrange("p (k n) -> p k n", k=KT_D) for s in range(2))
                w2_hi = whi[2][:].rearrange("p (k n) -> p k n", k=2)
                w2_lo = wlo[2][:].rearrange("p (k n) -> p k n", k=2)
                pe.wait_ge(lo_done, i * 3 + (F0_UNIT + 2))
                for st in range(6):
                    ch, ft = divmod(st, 2)
                    col, w = FF_CHUNKS[ch]
                    a, b = slice(ft * P, (ft + 1) * P), slice(col, col + w)
                    pe.wait_ge(gl_done, i * 6 + (st + 1))
                    for bank, w_hi, w_lo in ((2 * (st % 2), w1_hi, w1_lo), (2 * (st % 2) + 1, w3_hi, w3_lo)):
                        for k in range(KT_D):
                            last = three(ps[:, bank, 0:w], w_hi[:, k, a], w_lo[:, k, a], f_hi[:, k, b], f_lo[:, k, b],
                                         k == 0, k == KT_D - 1)
                    last.then_inc(step_pe, 1)
                pe.wait_ge(lo_done, i * 3 + (F0_UNIT + 3))
                for t in range(9):
                    rows = P if t < 8 else NS
                    ch = min(t // 3, 2)
                    if t % 3 == 0:
                        pe.wait_ge(gl_done, i * 6 + (2 * ch + 4))
                    for q in range(2):
                        m = 2 * t + q
                        pe.wait_ge(y_dve, i * 18 + (m + 1))
                        for k in range(2):
                            a, b = slice(t * P, t * P + rows), slice(512 * q, 512 * (q + 1))
                            last = three(ps[0:rows, 4 + m % 4, :], g_hi[:, k, a], g_lo[:, k, a],
                                         w2_hi[:, k, b], w2_lo[:, k, b], k == 0, k == 1)
                        last.then_inc(y_pe, 1)

            with pe.Fori(0, GROUPS - 1) as i:
                ffn_group(i)
            ffn_group(GROUPS - 1)


def _layout(inputs):
    import numpy as np

    f = {k: np.asarray(v) for k, v in inputs.items()}
    w_in = f["w_in"][0]
    starts = np.cumsum([0, HA * KA, HA * KA, HA * V, HA * V, RANK, HB * P, HB * P, HB * V])
    qa, ka, va, ga, lra, qb, fb, ib, gb = (int(s) for s in starts)

    def unit(w, rows, first, cols):
        part = w[:, first:first + cols]
        return np.ascontiguousarray(part.reshape(rows // P, P, cols).transpose(1, 0, 2)).reshape(P, -1)

    gate = [w_in[:, c + V * m:c + V * (m + 1)] for c, m in
            [(ga, n) if n < HA else (gb, n - HA) for n in ORDER]]
    wstream_a = np.stack([unit(w_in, D, c, 256) for c in (qa, qb, qb + 256, ka, fb, fb + 256)]
                         + [unit(np.concatenate(gate[m:m + 2], axis=1), D, 0, 256) for m in range(0, NH, 2)])
    low = np.zeros((P, KT_D, P), w_in.dtype)
    low[:, :, 0:RANK] = w_in[:, lra:lra + RANK].reshape(KT_D, P, RANK).transpose(1, 0, 2)
    v_cols = [va, va + 256, ib, ib + 256]
    w_o = f["w_o"][0].reshape(NH, V, D)[ORDER].reshape(NH * V, D)
    wstream_b = np.stack([unit(w_in, D, c, 256) for c in v_cols] + [unit(w_o, D, 256 * j, 256) for j in range(4)])
    w1, w3, w2 = f["w1"][0], f["w3"][0], f["w2"][0]
    wstream_f = np.stack([part for i in range(GROUPS) for part in (
        unit(w1, D, 256 * i, 256), unit(w3, D, 256 * i, 256), unit(w2[256 * i:256 * (i + 1)], 256, 0, D))])

    consts = np.zeros((P, C_ALL), np.float32)
    pos = np.arange(SC)
    consts[:, C_ID:C_ID + P] = np.eye(P)
    consts[:, C_ONE:C_ONE + P] = 1
    consts[:, C_CAUSAL:C_CAUSAL + P] = pos[:, None] <= pos[None, :]
    consts[:, C_M32:C_M32 + SLOTS * SC] = np.tile(pos % CH != 0, SLOTS)
    tok = np.arange(NS)
    consts[:, C_M8:C_M8 + SLOTS * NS] = np.tile(tok % ST != 0, SLOTS)
    same = tok[:, None] // ST == tok[None, :] // ST
    consts[0:NS, C_SMASK:C_SMASK + NS] = same & (tok[:, None] <= tok[None, :])
    consts[0:NS, C_BMASK:C_BMASK + SB] = tok[:, None] // ST == np.arange(SB)[None, :]

    def cols(v):
        return v.reshape(-1, P).T

    pvec = np.concatenate([cols(f["norm_mix"][0]), cols(f["norm_ffn"][0]), cols(f["b_a"][0]),
                           cols(f["lb_param"][0]), cols(f["lb_param"][1]), cols(f["onorm_a"][0]),
                           cols(f["onorm_b"][0])], axis=1)
    arrays = {
        "x_prompt": f["x_prompt"][0], "x_sample": f["x_sample"].reshape(NS, D),
        "state_gla": f["state_gla"][0], "state_hgrn": f["state_hgrn"][0],
        "wstream_a": wstream_a, "wstream_l": low.reshape(P, -1), "wstream_b": wstream_b, "wstream_f": wstream_f,
        "consts": consts, "pvec": pvec, "w_a2": f["w_a2"][0], "norm_final": f["norm_final"],
    }
    return {k: np.ascontiguousarray(v) for k, v in arrays.items()}


_OUTS = [("y_prompt", (SEQ, D)), ("y_sample", (NS, D)),
         ("new_gla_p", (HA, KA, V)), ("new_hgrn_p", (HB, P, V)),
         ("new_gla_s", (SB, HA, KA, V)), ("new_hgrn_s", (SB, HB, P, V))]


def kernel(**inputs):
    import concourse.bacc as bacc
    from concourse.bass_utils import run_bass_kernel_spmd

    nc = bacc.Bacc("TRN2", target_bir_lowering=False, num_devices=1)
    arrays = _layout(inputs)
    args = [nc.dram_tensor(f"in_{k}", a.shape, mybir.dt.from_np(a.dtype), kind="ExternalInput").ap()
            for k, a in arrays.items()]
    args += [nc.dram_tensor(f"out_{k}", s, F32, kind="ExternalOutput").ap() for k, s in _OUTS]
    build(nc, *args)
    r = run_bass_kernel_spmd(nc, [{f"in_{k}": a for k, a in arrays.items()}], core_ids=[0]).results[0]
    y_p, y_s, gla_p, hgrn_p, gla_s, hgrn_s = (r[f"out_{k}"] for k, _ in _OUTS)
    return (y_p.reshape(1, SEQ, D), y_s.reshape(SB, ST, D), gla_p[None, None], hgrn_p[None, None],
            gla_s[None], hgrn_s[None])
```

```python
from contextlib import ExitStack

import concourse.bass as bass
from concourse import mybir

F32 = mybir.dt.float32
F32R = mybir.dt.float32r
U32 = mybir.dt.uint32
ACT = mybir.ActivationFunctionType
ALU = mybir.AluOpType

P = 128
D = 1024
KT_D = D // P
SEQ = 1024
HALF = 512
SB, ST = 8, 8
NS = SB * ST
NTOK = SEQ + NS
HA, KA = 4, 64
HB = 4
NH = HA + HB
V = 128
RANK = 16
RANK2 = 2 * RANK
SLOTS = HA // 2 + HB
DFF = 2816
GROUPS = DFF // 256
CH = 32
SC = 128
NSC = HALF // SC
NCH = SC // CH
EPS = 1e-6
GATE_NORM = 16.0

A_UNITS, V_UNITS, O_UNITS = 10, 4, 4
L_UNIT = A_UNITS
L_SIZE = KT_D * RANK2
V0_UNIT = L_UNIT + 1
O0_UNIT = V0_UNIT + V_UNITS
HALF_UNITS = O0_UNIT + O_UNITS
F0_UNIT = 2 * HALF_UNITS
A_TILES = 2 * A_UNITS
QT, KTL, GT = 0, SLOTS, 2 * SLOTS
FT = KTL + HA // 2

C_ID, C_ONE, C_CAUSAL = 0, 128, 256
C_M32 = 384
C_M8 = C_M32 + SLOTS * SC
C_SMASK = C_M8 + SLOTS * NS
C_BMASK = C_SMASK + NS
C_ALL = C_BMASK + SB
V_GMIX, V_GFFN, V_BA, V_LB, V_ONA, V_ONB, V_ALL = 0, 8, 16, 18, 26, 27, 28

PLACE = [4, 5, 6, 7, 0, 1, 2, 3, 8]
FF_CHUNKS = [(0, 384), (384, 384), (768, 320)]


def half_tiles(h):
    tiles = [(PLACE[4 * h + j], P, j * P) for j in range(4)]
    return tiles + [(8, NS, HALF)] if h == 0 else tiles


OUT_TILES = [0, 1, 2, 3, 4, 5, 8, 6, 7]
FINAL_TILES = [0, 1, 2, 3, 4, 5, 6, 8, 7]

ORDER = [0, 2, 4, 5, 1, 3, 6, 7]


S_ORDER = [4, 5, 2, 3, 0, 1]
S_PIECES = [[1, 1, 2, 2, 0], [1, 1, 2, 2, 0]]


S_PLACES = [[0, 2, 1, 3], [4, 5, 6, 7]]


def piece(m):
    return S_ORDER[m // 2], 4 * (m % 2), (7, 3)[m % 2]


def head_place(n):
    return (n // 2, KA * (n % 2), KA) if n < HA else (n - HA + HA // 2, 0, P)


def build(nc, x_prompt, x_sample, state_gla, state_hgrn, wstream_a, wstream_l, wstream_b, wstream_f,
          consts, pvec, w_a2, norm_final,
          y_prompt, y_sample, new_gla_p, new_hgrn_p, new_gla_s, new_hgrn_s):
    with ExitStack() as ctx:
        def sem(name):
            return ctx.enter_context(nc.semaphore(name))

        def tensor(scope, name, shape, dt=F32):
            return scope.enter_context(nc.sbuf_tensor(name, shape, dt))

        con = tensor(ctx, "con", [P, C_ALL])
        pv = tensor(ctx, "pv", [P, V_ALL])
        wa2 = tensor(ctx, "wa2", [RANK2, HA * KA])
        x_res = tensor(ctx, "x_res", [P, 9, D])
        raw0 = tensor(ctx, "raw0", [P, 2048])
        whi = [tensor(ctx, f"whi{s}", [P, 2048], F32R) for s in range(2)]
        wlo = [tensor(ctx, f"wlo{s}", [P, 2048], F32R) for s in range(2)]
        small = tensor(ctx, "small", [P, 88])
        ms = small[:, 0:9]
        ms2 = small[:, 87:88]
        rs = small[:, 9:18]
        lb = small[:, 18:22]
        omlb = small[:, 22:26]
        lbw = small[:, 26:38].rearrange("p (a b) -> p a b", a=3)
        eps_t = small[:, 38:39]

        pscope = ExitStack()
        pr_main = tensor(pscope, "pr_main", [P, NSC, A_TILES, SC], F32R)
        tensor(pscope, "to_att", [P, A_TILES * NS + NSC * SLOTS * SC + SLOTS * NS + 5 * NH * V])
        pr_att = tensor(pscope, "pr_att", [P, NH, 2, NS], F32R)
        pscope.close()
        mix = ExitStack()
        p_main = tensor(mix, "p_main", [P, NSC, A_TILES, SC])
        p_samp = tensor(mix, "p_samp", [P, A_TILES, NS])
        b_main = tensor(mix, "b_main", [P, NSC, SLOTS, SC])
        b_samp = tensor(mix, "b_samp", [P, SLOTS, NS])
        val = tensor(mix, "val", [P, 5, NH * V])
        att = tensor(mix, "att", [P, 2, 4, SC])
        state = tensor(mix, "state", [P, SLOTS, V])
        fac = tensor(mix, "fac", [P, 2, SLOTS, 4 + 4 + 2 + 2 + 1 + 4])
        hscope = ExitStack()
        h_hi = tensor(hscope, "h_hi", [P, KT_D, HALF + NS], F32R)
        h_lo = tensor(hscope, "h_lo", [P, KT_D, HALF + NS], F32R)
        hscope.close()
        jscope = ExitStack()
        junk = tensor(jscope, "junk", [P, D])
        jscope.close()
        tscope = ExitStack()
        q_in, k_in, k_out, q_st, q_64, k_64 = [], [], [], [], [], []
        for j in (1, 0):
            for name, bufs, width in (("q_in", q_in, SC), ("k_in", k_in, SC), ("k_out", k_out, SC),
                                      ("q_st", q_st, SC), ("q_64", q_64, SC // 2), ("k_64", k_64, SC // 2)):
                bufs.insert(0, tensor(tscope, f"{name}{j}", [P, SLOTS, width]))
            if j == 1:
                kT_st = tensor(tscope, "kT_st", [P, SLOTS, SC])
            else:
                k_st = tensor(tscope, "k_st", [P, SLOTS, SC])
        tscope.close()
        mix.close()

        xscope = ExitStack()
        tensor(xscope, "p_main_place", [P, NSC * A_TILES * SC])
        f_xn = tensor(xscope, "f_xn", [P, 3, D])
        xscope.close()
        ffn = ExitStack()
        raw1 = tensor(ffn, "raw1", [P, 2048])
        yscope = ExitStack()
        f_xn3 = tensor(yscope, "f_xn3", [P, 4, D])
        yscope.close()
        whi.append(tensor(ffn, "whi2", [P, 2048], F32R))
        wlo.append(tensor(ffn, "wlo2", [P, 2048], F32R))
        gated = tensor(ffn, "gated", [P, 2, 384])
        nf = tensor(ffn, "nf", [P, D])
        g_hi = tensor(ffn, "g_hi", [P, 2, SEQ], F32R)
        g_lo = tensor(ffn, "g_lo", [P, 2, SEQ], F32R)
        g_samp = tensor(ffn, "g_samp", [P, 2, 2, NS], F32R)
        tensor(ffn, "f_gap", [P, 1616])
        f_hi = tensor(ffn, "f_hi", [P, KT_D, NTOK], F32R)
        f_lo = tensor(ffn, "f_lo", [P, KT_D, NTOK], F32R)
        ffn.close()

        lr_t = [x_res[0:RANK2, 6, 0:HALF + NS], val[0:RANK2, 4, 0:HALF]]
        az_s = x_res[:, 7, 0:2 * NS].rearrange("p (a t) -> p a t", a=2)
        az_m = att[:].rearrange("p g n t -> p (g n t)").rearrange("p (c a t) -> p c a t", c=NSC, a=2)
        s_state = x_res[:, 0:SLOTS, :].rearrange("p s (b v) -> p s b v", b=SB)
        b_flat = b_main[:, 0:2].rearrange("p c s t -> p (c s t)")
        sq_in, sk_in, sk_out = (b_flat[:, m * SLOTS * NS:(m + 1) * SLOTS * NS].rearrange("p (s t) -> p s t", s=SLOTS)
                                for m in range(3))
        sq_pair = b_flat[:, 3 * SLOTS * NS:3 * SLOTS * NS + HA * NS].rearrange(
            "p (s b e t) -> p s b e t", s=HA // 2, b=SB, e=2)
        k_place = [p_main[:, c, KTL + 2:KTL + 6, :] for c in range(NSC)]
        s_att = k_place[0].rearrange("p a t -> p (a t)").rearrange("p (n t) -> p n t", n=NH)
        skT = b_main[0:NS, 2]
        skm = [k_place[1][0:NS], k_place[2][0:NS]]

        ps = ctx.enter_context(nc.psum_tensor("ps", [P, 8, 512], F32))

        raw_one = p_main[:, NSC - 1].rearrange("p a t -> p (a t)")[:, 0:2048]

        ident = con[:, C_ID:C_ID + P]
        ones = con[:, C_ONE:C_ONE + P]
        causal = con[:, C_CAUSAL:C_CAUSAL + P].bitcast(U32)
        m32 = con[:, C_M32:C_M32 + SLOTS * SC]
        m8 = con[:, C_M8:C_M8 + SLOTS * NS]
        smask = con[0:NS, C_SMASK:C_SMASK + NS].bitcast(U32)
        bmask = con[0:NS, C_BMASK:C_BMASK + SB]
        fq = [fac[:, j, :, 0:4] for j in range(2)]
        gk = [fac[:, j, :, 4:8] for j in range(2)]
        f64 = [fac[:, j, :, 8:10] for j in range(2)]
        g64 = [fac[:, j, :, 10:12] for j in range(2)]
        dtot = [fac[:, j, :, 12:13] for j in range(2)]
        ech = [fac[:, j, :, 13:17] for j in range(2)]
        dsamp = small[:, 39:39 + SLOTS * SB].rearrange("p (s b) -> p s b", s=SLOTS)

        id_ld, pv_ld, c_ld = sem("ident_loaded"), sem("pvec_loaded"), sem("consts_loaded")
        x0_ld = sem("x_loaded_tile0")
        x_ld = [sem("x_loaded_tile1"), sem("x_loaded_pair1"), sem("x_loaded_sample"), sem("x_loaded_half1")]
        h_lo_used = sem("h_lo_used")
        half_done = sem("weights_hi_first_half")
        one_ld = sem("unit_1_loaded")
        paired = sem("low_rank_parts_paired")
        xr_ld = sem("x_reloaded")
        raw0_ld, raw1_ld = sem("raw0_loaded"), sem("raw1_loaded")
        st_ld = sem("sample_states_loaded")
        nf_ld = sem("norm_final_loaded")
        out_st = sem("outputs_stored")
        lb_e, lb_v = sem("lb_exp"), sem("lb_vector")
        eps_set = sem("eps_set")
        sq_done, lnms_done = sem("squares_done"), sem("ln_mean_done")
        rs_done, xn_done = sem("rstd_done"), sem("xn_done")
        tr_done, th_done, tl_done = sem("transposed"), sem("turned_hi"), sem("turned_lo")
        hi_done, lo_done, used = sem("weights_hi"), sem("weights_lo"), sem("unit_used")
        ev_a, ev_v = sem("unit_evacuated_act"), sem("unit_evacuated_dve")
        z_pe, z_dve = sem("z_product"), sem("z_biased")
        silu_done, sig_done, f_done, lnf_done, k_done = (
            sem("silu_done"), sem("sigmoid_done"), sem("forget_done"), sem("log_forget_done"), sem("k_done"))
        az_done, aze_done, azl_done, zm_done, la_done = (
            sem("abs_z_done"), sem("exp_abs_z"), sem("ln1p_done"), sem("min_z_done"), sem("log_alpha_done"))
        la2_done, b_done, g_done, qs_done = sem("log_decay_done"), sem("cumsum_done"), sem("gate_scaled"), sem("q_scaled")
        zero_att, zero_state, ones_fac = sem("att_zeroed"), sem("state_zeroed"), sem("factors_set")
        e1_done, e3_done = sem("exp_b_done"), sem("exp_d_done")
        d_done, prep1_done, prep_done = sem("d_done"), sem("q_k_decayed"), sem("prep_done")
        fac_a, fac_b, pool_q, pool_k = sem("factors_a"), sem("factors_b"), sem("pool_q_done"), sem("pool_k_done")
        kt_pe, kt_act = sem("k_transposed"), sem("kT_copied")
        att_pe, att_dve = sem("scores_done"), sem("scores_masked")
        kv_pe, st_done = sem("kv_done"), sem("state_updated")
        o_pe, o_act, osq_act = sem("o_done"), sem("o_copied"), sem("o_squared")
        ss_pe, ln_act, rn_act = sem("sumsq_done"), sem("ln_ms_done"), sem("rstd_o_done")
        on_dve, og_pool, og_dve = sem("o_normed"), sem("o_gated"), sem("last_o_gated")
        oh_act, ol_dve = sem("o_hi_done"), sem("o_lo_done")
        s_b, s_e1, s_d, s_e3, s_prep = sem("s_cumsum"), sem("s_exp_b"), sem("s_d"), sem("s_exp_d"), sem("s_prep")
        s_zero, s_att_pe, s_att_dve = sem("s_att_zeroed"), sem("s_scores_done"), sem("s_scores_masked")
        s_t, s_dm, s_kv = sem("s_transposed"), sem("s_kT_masked"), sem("s_kv_done")
        s_q, s_pair = sem("s_q_decayed"), sem("s_q_paired")
        s_tc, s_upd = sem("s_kT_copied"), sem("s_state_updated")
        s_o, s_ocp, s_osq, s_ss = sem("s_o_done"), sem("s_o_copied"), sem("s_o_squared"), sem("s_sumsq_done")
        s_ln, s_rn, s_on, s_og = sem("s_ln_ms_done"), sem("s_rstd_o_done"), sem("s_o_normed"), sem("s_o_gated")
        z_s_pe, z_s_dve = sem("s_z_product"), sem("s_z_biased")
        ms_dve = sem("last_squares_added")
        fold_act, fold_dve = sem("sample_upper_copied"), sem("sample_folded")
        step_pe, silu_f, gm_done, gh_done, gl_done = (
            sem("ffn_step_done"), sem("ffn_silu"), sem("ffn_gated"), sem("ffn_g_hi"), sem("ffn_g_lo"))
        y_pe, y_dve = sem("ffn_out_done"), sem("ffn_out_added")
        sqf, lnf, rsf, yf_done = (
            sem("final_squares"), sem("final_ln_mean"), sem("final_rstd"), sem("final_y"))

        block = ctx.enter_context(nc.Block())

        def half(h, size=NS):
            return size if h == 0 else 0

        @block.sync
        def _(sp):
            def load_pair(p):
                for t in (2 * p, 2 * p + 1):
                    sp.dma_start(x_res[:, PLACE[t], :], x_prompt[t * P:(t + 1) * P, :]).then_inc(
                        x_ld[p] if t else x0_ld, 16)

            load_pair(0)
            sp.dma_start(con[:, 0:C_M32], consts[:, 0:C_M32]).then_inc(id_ld, 16)
            sp.dma_start(raw0[:], wstream_a[0]).then_inc(raw0_ld, 16)
            sp.dma_start(pv[:], pvec).then_inc(pv_ld, 16)
            load_pair(1)
            sp.dma_start(x_res[0:NS, 8, :], x_sample).then_inc(x_ld[2], 16)
            sp.dma_start(raw_one, wstream_a[1]).then_inc(one_ld, 16)

            def load_unit(u, src, size=2048):
                sp.wait_ge(lo_done, u if u > 2 else 1)
                sp.dma_start(raw0[:, 0:size], src).then_inc(raw0_ld, 16)

            def sample_states():
                sp.wait_ge(xn_done, 5)
                for p in range(2):
                    for e in range(2):
                        sp.dma_start(s_state[KA * e:KA * (e + 1), p],
                                     state_gla[:, 2 * p + e].rearrange("b k v -> k b v")).then_inc(st_ld, 16)
                for n in range(HB):
                    sp.dma_start(s_state[:, 2 + n],
                                 state_hgrn[:, n].rearrange("b k v -> k b v")).then_inc(st_ld, 16)

            def store_sample_states(places):
                for place in places:
                    slot = S_ORDER[place]
                    sp.wait_ge(s_upd, 2 * (place + 1))
                    for n in range(NH):
                        sl, lo, kw = head_place(n)
                        if sl == slot:
                            dst = new_gla_s[:, n] if n < HA else new_hgrn_s[:, n - HA]
                            sp.dma_start(dst.rearrange("b k v -> k b v"),
                                         s_state[lo:lo + kw, slot]).then_inc(out_st, 16)

            def reload_x(tiles):
                for t in tiles:
                    sp.dma_start(x_res[:, PLACE[t], :], x_prompt[t * P:(t + 1) * P, :]).then_inc(xr_ld, 16)

            def load_o(u0, r):
                load_unit(u0 + O0_UNIT + r, wstream_b[V_UNITS + r])

            for h in range(2):
                u0 = h * HALF_UNITS
                for r in range(O0_UNIT):
                    u = u0 + r
                    if u < 2:
                        continue
                    if u == 2:
                        sp.dma_start(con[:, C_M32:], consts[:, C_M32:]).then_inc(c_ld, 16)
                        for part in range(2):
                            sp.dma_start(wa2[part * RANK:(part + 1) * RANK, :], w_a2).then_inc(c_ld, 16)
                    if r < A_UNITS:
                        load_unit(u, wstream_a[r])
                    elif r == L_UNIT:
                        load_unit(u, wstream_l, L_SIZE)
                    else:
                        load_unit(u, wstream_b[r - V0_UNIT])
                    if h == 0 and r == 3:
                        sample_states()
                load_o(u0, 0)
                load_o(u0, 1)
                if h == 0:
                    sp.wait_ge(la_done, 1)
                    reload_x([2, 3])
                    sp.wait_ge(o_pe, 2 * NSC)
                    for j in range(4):
                        t = 4 + j
                        sp.dma_start(val[:, j, :], x_prompt[t * P:(t + 1) * P, :]).then_inc(x_ld[3], 16)
                    load_o(u0, 2)
                    store_sample_states([0, 1])
                    sp.wait_ge(out_st, 16 * 2)
                    sp.wait_ge(xr_ld, 16 * 2)
                    reload_x([0, 1])
                    load_o(u0, 3)
                    store_sample_states([2, 3, 4, 5])
                    sp.wait_ge(out_st, 16 * NH)
                    reload_x([4, 5, 6, 7])
                else:
                    sp.wait_ge(st_done, 2 * NSC)
                    for p in range(2):
                        for e in range(2):
                            sp.dma_start(new_gla_p[2 * p + e],
                                         state[KA * e:KA * (e + 1), p, :]).then_inc(out_st, 16)
                    for n in range(HB):
                        sp.dma_start(new_hgrn_p[n], state[:, 2 + n, :]).then_inc(out_st, 16)
                    load_o(u0, 2)
                    load_o(u0, 3)

            for part in range(3):
                sp.wait_ge(lo_done, F0_UNIT + part)
                sp.dma_start(raw0[:], wstream_f[part]).then_inc(raw0_ld, 16)
            sp.wait_ge(used, F0_UNIT)
            sp.dma_start(nf[:], norm_final.partition_broadcast(P)).then_inc(nf_ld, 16)
            with sp.Fori(1, GROUPS) as i:
                sp.wait_ge(lo_done, i * 3 + F0_UNIT)
                sp.dma_start(raw0[:], wstream_f[bass.ds(i * 3, 1)].rearrange("u p c -> p (u c)")).then_inc(raw0_ld, 16)
                sp.dma_start(raw1[:], wstream_f[bass.ds(i * 3 + 1, 1)].rearrange("u p c -> p (u c)")).then_inc(raw1_ld, 16)
                sp.wait_ge(lo_done, i * 3 + F0_UNIT + 1)
                sp.dma_start(raw0[:], wstream_f[bass.ds(i * 3 + 2, 1)].rearrange("u p c -> p (u c)")).then_inc(raw0_ld, 16)
            for n, t in enumerate(FINAL_TILES):
                sp.wait_ge(yf_done, n + 1)
                if t == 8:
                    sp.dma_start(y_sample, x_res[0:NS, 8, :]).then_inc(out_st, 16)
                elif n < 8:
                    sp.dma_start(y_prompt[t * P:(t + 1) * P, :], x_res[:, PLACE[t], :]).then_inc(out_st, 16)
                else:
                    for q in range(2):
                        sp.wait_ge(yf_done, n + 1 + q)
                        cols = slice(512 * q, 512 * (q + 1))
                        sp.dma_start(y_prompt[t * P:(t + 1) * P, cols], x_res[:, PLACE[t], cols]).then_inc(out_st, 16)
            sp.wait_ge(out_st, 2 * 16 * NH + 16 * 10)

        def act_copies_before(u):
            h, r = divmod(u, HALF_UNITS)
            return O0_UNIT * h + min(r, O0_UNIT)

        def slot_of(u):
            return u % 2 if u < F0_UNIT else (u - F0_UNIT) % 3

        IN_HALVES = [0, V0_UNIT, HALF_UNITS + V0_UNIT]

        def raw_of(u):
            return raw_one if u == 1 else raw0

        @block.gpsimd
        def _(pool):
            nc.gpsimd.memset(eps_t, EPS).then_inc(eps_set, 1)
            nc.gpsimd.memset(fac[:], 1.0).then_inc(ones_fac, 1)
            nc.gpsimd.memset(state[:], 0.0).then_inc(zero_state, 1)
            for h in range(2):
                pool.wait_ge(lo_done, HALF_UNITS * h + L_UNIT + 1)
                s = slot_of(HALF_UNITS * h + L_UNIT)
                hi, lo = (w[s][:, 0:L_SIZE].rearrange("p (k n) -> p k n", k=KT_D)[:, :, RANK:RANK2]
                          for w in (whi, wlo))
                nc.gpsimd.tensor_copy(hi, lo).then_inc(paired, 1)
                pool.wait_ge(ev_v, HALF_UNITS * h + L_UNIT + 3)
                pool.wait_ge(ev_a, 2 + act_copies_before(HALF_UNITS * h + L_UNIT))
                parts = [p_main[:, :, 0:2, :]] + ([p_samp[:, 0:2, :]] if h == 0 else [])
                for part in parts:
                    last = nc.gpsimd.tensor_scalar(part, part, KA ** -0.5, None, ALU.mult)
                last.then_inc(qs_done, 1)
                pool.wait_ge(silu_done, 4 if h == 0 else 6)
                for a, col in ((GT, V_ONA), (GT + 2, V_ONB), (GT + 4, V_ONA), (GT + 6, V_ONB)):
                    gs = [p_main[:, :, a:a + 2, :]] + ([p_samp[:, a:a + 2, :]] if h == 0 else [])
                    for g in gs:
                        last = nc.gpsimd.tensor_scalar(g, g, pv[:, col:col + 1], None, ALU.mult)
                last.then_inc(g_done, 1)
                pool.wait_ge(la_done, h + 1)
                nc.gpsimd.memset(att[:], 0.0).then_inc(zero_att, 1)

                def gate(C):
                    c = C % NSC
                    pool.wait_ge(on_dve, 2 * (C + 1))
                    pool.wait_ge(g_done, C // NSC + 1)
                    o = p_main[:, c, 0:NH, :]
                    nc.gpsimd.tensor_tensor(o, o, p_main[:, c, GT:GT + NH, :], ALU.mult).then_inc(og_pool, 1)

                for c in range(NSC):
                    C = NSC * h + c
                    j = C % 2
                    pool.wait_ge(e1_done, 3 * (C + 1))
                    if C == 0:
                        pool.wait_ge(ones_fac, 1)
                    if C >= 2:
                        pool.wait_ge(st_done, C - 1)
                        pool.wait_ge(prep_done, C - 1)
                        pool.wait_ge(pool_k, C - 1)
                        pool.wait_ge(pool_q, C - 1)
                    nc.gpsimd.tensor_copy(fq[j][:, :, 1:2], ech[j][:, :, 0:1])
                    nc.gpsimd.tensor_tensor(fq[j][:, :, 2:3], ech[j][:, :, 0:1], ech[j][:, :, 1:2], ALU.mult)
                    nc.gpsimd.tensor_copy(gk[j][:, :, 2:3], ech[j][:, :, 3:4])
                    nc.gpsimd.tensor_tensor(gk[j][:, :, 1:2], ech[j][:, :, 3:4], ech[j][:, :, 2:3], ALU.mult)
                    nc.gpsimd.tensor_copy(g64[j][:, :, 0:1], ech[j][:, :, 1:2])
                    nc.gpsimd.tensor_copy(f64[j][:, :, 1:2], ech[j][:, :, 2:3]).then_inc(fac_a, 1)
                    pool.wait_ge(fac_a, C + 1)
                    nc.gpsimd.tensor_tensor(fq[j][:, :, 3:4], fq[j][:, :, 2:3], ech[j][:, :, 2:3], ALU.mult)
                    nc.gpsimd.tensor_tensor(gk[j][:, :, 0:1], gk[j][:, :, 1:2], ech[j][:, :, 1:2], ALU.mult)
                    nc.gpsimd.tensor_tensor(dtot[j], fq[j][:, :, 2:3], gk[j][:, :, 1:2], ALU.mult).then_inc(fac_b, 1)
                    pool.wait_ge(fac_b, C + 1)
                    pool.wait_ge(prep1_done, C + 1)
                    if C >= 1:
                        pool.wait_ge(kt_pe, C)
                    nc.gpsimd.tensor_tensor(
                        k_st[:].rearrange("p s (c t) -> p s c t", c=NCH),
                        k_out[j][:].rearrange("p s (c t) -> p s c t", c=NCH),
                        gk[j].unsqueeze(3).broadcast_to((P, SLOTS, NCH, CH)), ALU.mult).then_inc(pool_k, 1)
                    if C >= 2:
                        pool.wait_ge(o_pe, 2 * (C - 1))
                    nc.gpsimd.tensor_tensor(
                        q_st[j][:].rearrange("p s (c t) -> p s c t", c=NCH),
                        q_in[j][:].rearrange("p s (c t) -> p s c t", c=NCH),
                        fq[j].unsqueeze(3).broadcast_to((P, SLOTS, NCH, CH)), ALU.mult).then_inc(pool_q, 1)
                    if c >= 2:
                        gate(C - 2)
                if h == 0:
                    nc.gpsimd.memset(s_att, 0.0)
                    nc.gpsimd.memset(sq_pair, 0.0).then_inc(s_zero, 1)
                gate(NSC * h + 2)
                if h == 0:
                    pool.wait_ge(s_on, 1)
                    nc.gpsimd.tensor_tensor(p_samp[:, 0:NH, :], p_samp[:, 0:NH, :],
                                            p_samp[:, GT:GT + NH, :], ALU.mult).then_inc(s_og, 1)

        def wide(ap):
            return ap.rearrange("p (a d) -> p a d", a=2)

        def stage_parts(n):
            holes = [p_main[:, 2 * m:2 * m + 2, KTL + 2:KTL + 6, :].rearrange("p c a t -> p c (a t)")
                     for m in range(2)]
            first = PLACE[4 * (n % 2)]
            scratch = {0: [wide(val[:, j, :]) for j in range(4)],
                       1: [wide(val[:, j, :]) for j in range(4)],
                       2: [wide(f_xn[:, j, :]) for j in range(3)] + [holes[0]],
                       3: [wide(f_xn3[:, j, :]) for j in range(4)]}[n]
            main = [(first + j, P, scratch[j] if n == 1 else wide(x_res[:, first + j, :]), scratch[j])
                    for j in range(4)]
            s_scratch = {0: wide(val[0:NS, 4, :]), 2: holes[1][0:NS]}.get(n)
            samp = (8, NS, wide(x_res[0:NS, 8, :]), s_scratch) if s_scratch is not None else None
            hi, lo = (h_hi, h_lo) if n < 2 else (f_hi, f_lo)
            return main, samp, hi, lo, HALF if n == 3 else 0, HALF if n == 0 else SEQ, V_GMIX if n < 2 else V_GFFN

        N_STAGES = 4

        def turn_bank(n, k):
            return [1, (3, 7)[k % 2], (3, 7)[k % 2], 4 + k % 4][n]

        def tiles_before(n):
            return sum(len(stage_parts(m)[0]) + bool(stage_parts(m)[1]) for m in range(n))

        def turns_before(n):
            return sum(KT_D * bool(stage_parts(m)[0]) + bool(stage_parts(m)[1]) for m in range(n))

        def row_groups(n):
            main, samp = stage_parts(n)[:2]
            first = main[0][0]
            pieces = [(first, 2, P), (first + 2, 2, P)] if n == 0 else [(first, 4, P)]
            return pieces + ([(8, 1, NS)] if samp else [])

        def groups_before(n):
            return sum(len(row_groups(m)) for m in range(n))

        def first_tiles(group):
            main, samp = stage_parts(0)[:2]
            return (main + [samp])[2 * group:2 * group + 2]

        def sum_place(C, g, samp=False):
            if samp:
                return p_samp[:, KTL + 2:KTL + 6, :] if g == 0 else b_samp[:, 0:4, :]
            c = C % NSC
            return p_main[:, c, KTL + 2:KTL + 6, :] if g == 0 else b_main[:, c, 0:4, :]

        def turns_at(h, r):
            none = [None] * 4
            return [[none, none], [none, [None, None, 0, 1]], [[0, 1, 2, 3], [2, 3, 4, 5]],
                    [[4, 5, 6, 7], [6, 7, 8, None]]][r][h]

        def s_tiles(g, first=0):
            return p_samp[:, first:first + NH, :].rearrange("p (a b) t -> p a b t", b=4)[:, :, 2 * g:2 * g + 2, :]

        def by_two(ap):
            return ap.rearrange("p (a b) t -> p a b t", a=2)

        def kT_bank(c):
            return 2 if c else 6

        def split_count(C):
            return C + 1 if C < NSC else C + 2

        @block.scalar
        def _(act):
            act.preload_act_table_set("natural_log_exp_and_others")

            def split_hi(u):
                size = L_SIZE if u % HALF_UNITS == L_UNIT else 2048
                if u == 1:
                    act.wait_ge(one_ld, 16)
                else:
                    act.wait_ge(raw0_ld, 16 * max(u, 1))
                if u >= 2:
                    act.wait_ge(used, u - 1)
                s = slot_of(u)
                first = 0
                if u in IN_HALVES:
                    first = 1024
                    nc.scalar.activation(whi[s][:, 0:first], raw_of(u)[:, 0:first], ACT.Copy).then_inc(half_done, 1)
                nc.scalar.activation(whi[s][:, first:size], raw_of(u)[:, first:size], ACT.Copy).then_inc(hi_done, 1)

            def inverse_root(stat, to, ln_sem, count, done):
                rows = stat.shape[0]
                nc.scalar.activation(stat, stat, ACT.Ln, scale=1.0 / D, bias=eps_t[0:rows]).then_inc(ln_sem, 1)
                act.wait_ge(ln_sem, count)
                nc.scalar.activation(to, stat, ACT.Exp, scale=-0.5).then_inc(done, 1)

            def squares(n):
                main, samp = stage_parts(n)[:2]
                if n == 1:
                    act.wait_ge(x_ld[3], 16 * 4)
                if n == 2:
                    act.wait_ge(on_dve, 4 * NSC)
                if n == 3:
                    act.wait_ge(ev_v, F0_UNIT + 2)
                cnt = tiles_before(n)
                for m, (place, rows, x, scratch) in enumerate(main + ([samp] if samp else [])):
                    if n == 1:
                        scratch = wide(junk[:])
                        if m:
                            act.wait_ge(sq_done, cnt + m)
                    nc.scalar.activation(scratch, x, ACT.Square,
                                         accum_out=ms[0:rows, place:place + 1]).then_inc(sq_done, 1)
                for m, (place, num, rows) in enumerate(row_groups(n)):
                    act.wait_ge(sq_done, cnt + (num if m == 0 else tiles_before(n + 1) - cnt))
                    inverse_root(ms[0:rows, place:place + num], rs[0:rows, place:place + num],
                                 lnms_done, groups_before(n) + m + 1, rs_done)

            def first_squares(group):
                tiles = first_tiles(group)
                for m, (place, rows, x, scratch) in enumerate(tiles):
                    if group == 0 and m == 0:
                        act.wait_ge(x0_ld, 16)
                    else:
                        act.wait_ge(x_ld[group], 16 * (1 if group == 0 else len(tiles)))
                    nc.scalar.activation(scratch, x, ACT.Square,
                                         accum_out=ms[0:rows, place:place + 1]).then_inc(sq_done, 1)
                place, num, rows = row_groups(0)[group]
                act.wait_ge(sq_done, 2 * group + num)
                inverse_root(ms[0:rows, place:place + num], rs[0:rows, place:place + num],
                             lnms_done, group + 1, rs_done)

            def first_hi(p, kk):
                act.wait_ge(tr_done, 4 * p + kk + 1)
                for e in range(2):
                    k = 2 * kk + e
                    last = nc.scalar.activation(h_hi[:, k, 256 * p:256 * (p + 1)],
                                                ps[:, 2 * kk + 1, 256 * e:256 * (e + 1)], ACT.Copy,
                                                scale=pv[:, V_GMIX + k:V_GMIX + k + 1])
                last.then_inc(th_done, 1)

            def turned_hi(n, k):
                main, samp, hi, lo, mcol, scol, gain = stage_parts(n)
                act.wait_ge(tr_done, turns_before(n) + k + 1)
                bank = turn_bank(n, k)
                if n == 2 and k == 0:
                    act.wait_ge(out_st, 2 * 16 * NH)
                if k < KT_D:
                    last = nc.scalar.activation(hi[:, k, mcol:mcol + HALF], ps[:, bank, :], ACT.Copy,
                                                scale=pv[:, gain + k:gain + k + 1])
                else:
                    for m in range(KT_D):
                        last = nc.scalar.activation(hi[:, m, scol:scol + NS], ps[:, bank, m * NS:(m + 1) * NS],
                                                    ACT.Copy, scale=pv[:, gain + m:gain + m + 1])
                last.then_inc(th_done, 1)

            def fold(scratch):
                nc.scalar.activation(scratch, x_res[NS:P, 8, :], ACT.Copy).then_inc(fold_act, 1)

            def out_hi(C):
                c = C % NSC
                if c < NSC - 1:
                    act.wait_ge(og_pool, (NSC - 1) * (C // NSC) + c + 1)
                else:
                    act.wait_ge(on_dve, 2 * (C + 1))
                nc.scalar.activation(pr_main[:, c, GT:GT + NH, :], p_main[:, c, 0:NH, :],
                                     ACT.Copy).then_inc(oh_act, 1)

            def exps(C):
                c, j = C % NSC, C % 2
                act.wait_ge(b_done, C + 1)
                if c == 0:
                    act.wait_ge(h_lo_used, C // NSC + 1)
                else:
                    act.wait_ge(used, HALF_UNITS * (C // NSC) + O0_UNIT)
                if C == 0:
                    act.wait_ge(ones_fac, 1)
                if C >= 2:
                    act.wait_ge(o_pe, 2 * (C - 1))
                    act.wait_ge(pool_q, C - 1)
                    act.wait_ge(fac_b, C - 1)
                b = b_main[:, c]
                ends = b.rearrange("p s (c t) -> p s c t", c=NCH)[:, :, :, CH - 1:CH]
                nc.scalar.activation(q_in[j][:], b, ACT.Exp).then_inc(e1_done, 1)
                nc.scalar.activation(k_in[j][:], b, ACT.Exp, scale=-1.0).then_inc(e1_done, 1)
                nc.scalar.activation(ech[j].unsqueeze(3), ends, ACT.Exp).then_inc(e1_done, 1)

            def exp_d(C):
                j = C % 2
                act.wait_ge(d_done, C + 1)
                nc.scalar.activation(k_out[j][:], k_out[j][:], ACT.Exp).then_inc(e3_done, 1)

            def rstd(C, g, bank, count, ln_sem, rn_sem, width, samp=False):
                place = sum_place(C, g, samp)
                nc.scalar.activation(place, bank, ACT.Ln, scale=1.0 / V, bias=eps_t).then_inc(ln_sem, 1)
                act.wait_ge(ln_sem, count)
                nc.scalar.activation(place, place, ACT.Exp, scale=-0.5).then_inc(rn_sem, 1)

            def rstd_main(C):
                for g in range(2):
                    act.wait_ge(ss_pe, 2 * C + g + 1)
                    rstd(C, g, ps[:, 2 + g, :].rearrange("p (n t) -> p n t", n=4), 2 * C + g + 1,
                         ln_act, rn_act, SC)

            def copy_o(C):
                c = C % NSC
                for g in range(2):
                    act.wait_ge(o_pe, 2 * C + g + 1)
                    o = ps[:, 6 + g, :].rearrange("p (n t) -> p n t", n=4)
                    nc.scalar.activation(p_main[:, c, 4 * g:4 * g + 4, :], o, ACT.Copy).then_inc(o_act, 1)
                    nc.scalar.activation(sum_place(C, g), o, ACT.Square).then_inc(osq_act, 1)

            act.sem_inc(ev_a, 2)
            for h in range(2):
                u0 = HALF_UNITS * h
                bc = (h == 0)

                def evacuate(i, e):
                    u = u0 + e
                    act.wait_ge(used, i * 2 + (u + 1))
                    b0 = 4 * (u % 2)
                    tile = i * 4 + 2 * e
                    for q in range(2):
                        src = ps[:, b0 + q, 0:256].rearrange("p (c o t) -> p c o t", c=2, o=1)
                        last = nc.scalar.activation(p_main[:, 2 * q:2 * q + 2, bass.ds(tile, 1), :], src, ACT.Copy)
                    if h == 0:
                        src = ps[:, b0 + 1, 256:256 + NS].unsqueeze(1)
                        last = nc.scalar.activation(p_samp[:, bass.ds(tile, 1), :], src, ACT.Copy)
                    last.then_inc(ev_a, 1)

                if h == 0:
                    act.wait_ge(eps_set, 1)
                    first_squares(0)
                    split_hi(0)
                    act.wait_ge(pv_ld, 16)
                    for kk in range(4):
                        first_hi(0, kk)
                    first_squares(1)
                    split_hi(1)
                    first_squares(2)
                    for kk in range(4):
                        first_hi(1, kk)
                    turned_hi(0, KT_D)
                    act.wait_ge(lb_v, 1)
                    nc.scalar.activation(lbw[:, 0:2, :], lbw[:, 0:2, :], ACT.Exp).then_inc(lb_e, 1)
                    evacuate(0, 0)
                    split_hi(2)
                    evacuate(0, 1)
                else:
                    act.wait_ge(used, u0)
                    act.wait_ge(ev_v, HALF_UNITS + 2)
                    fold(val[0:NS, 4, :])
                with act.Fori(1 - h, A_UNITS // 2) as i:
                    for e in range(2):
                        u = u0 + e
                        s = slot_of(u + 1)
                        act.wait_ge(raw0_ld, i * 32 + 16 * (u + 1))
                        nc.scalar.activation(whi[s][:], raw0[:], ACT.Copy).then_inc(hi_done, 1)
                        evacuate(i, e)
                u = u0 + L_UNIT
                split_hi(u + 1)
                act.wait_ge(used, u + 1)
                nc.scalar.activation(lr_t[h][:, 0:256], ps[0:RANK2, 4 * (u % 2), 0:256], ACT.Copy).then_inc(ev_a, 1)

                def split_after(v):
                    split_hi(u0 + V0_UNIT + v + 1)

                def values(v):
                    u = u0 + V0_UNIT + v
                    act.wait_ge(used, u + 1)
                    for t in range(2):
                        last = nc.scalar.activation(val[:, t, 256 * v:256 * (v + 1)],
                                                    ps[:, 4 * (u % 2), 256 * t:256 * (t + 1)], ACT.Copy)
                    last.then_inc(ev_a, 1)

                split_after(0)
                act.wait_ge(ev_v, u0 + L_UNIT + 3)
                act.wait_ge(ev_a, 2 + act_copies_before(u0 + V0_UNIT))
                parts = [p_main[:, :, FT:FT + HB, :]] + ([p_samp[:, FT:FT + HB, :]] if bc else [])
                for part in parts:
                    nc.scalar.activation(part, part, ACT.Sigmoid).then_inc(sig_done, 1)
                parts = [p_main[:, :, 2:6, :]] + ([p_samp[:, 2:6, :]] if bc else [])
                for part in parts:
                    nc.scalar.activation(part, part, ACT.Silu).then_inc(silu_done, 1)
                values(0)
                split_after(1)
                parts = [p_main[:, :, GT:A_TILES, :]] + ([p_samp[:, GT:A_TILES, :]] if bc else [])
                for part in parts:
                    nc.scalar.activation(part, part, ACT.Silu).then_inc(silu_done, 1)
                values(1)
                act.preload_act_table_set("natural_log_exp_and_others")
                split_after(2)
                act.wait_ge(z_dve, h + 1)
                if bc:
                    act.wait_ge(z_s_dve, 1)
                azs = [(az_m, b_main[:, :, 0:2, :])] + ([(az_s, b_samp[:, 0:2, :])] if bc else [])
                base = 0 if h == 0 else 2
                for n, (az, z) in enumerate(azs):
                    nc.scalar.activation(az, z, ACT.Abs).then_inc(az_done, 1)
                    act.wait_ge(az_done, base + n + 1)
                    nc.scalar.activation(az, az, ACT.Exp, scale=-1.0).then_inc(aze_done, 1)
                    act.wait_ge(aze_done, base + n + 1)
                    nc.scalar.activation(az, az, ACT.Ln, bias=ones[:, 0:1]).then_inc(azl_done, 1)
                act.wait_ge(f_done, h + 1)
                nc.scalar.activation(b_main[:, :, 2:6, :], p_main[:, :, FT:FT + HB, :], ACT.Ln).then_inc(lnf_done, 1)
                if bc:
                    nc.scalar.activation(b_samp[:, 2:6, :], p_samp[:, FT:FT + HB, :], ACT.Ln).then_inc(lnf_done, 1)
                values(2)
                C0 = NSC * h
                exps(C0)
                exp_d(C0)
                values(3)
                for c in range(NSC):
                    C = C0 + c
                    if c + 1 < NSC:
                        exps(C + 1)
                    act.wait_ge(kt_pe, C + 1)
                    if C >= 1:
                        act.wait_ge(kv_pe, C)
                    if c == 0:
                        act.wait_ge(used, u0 + O0_UNIT)
                    nc.scalar.activation(kT_st[:, 0:4, :], ps[:, kT_bank(c), :].rearrange("p (s t) -> p s t", s=4), ACT.Copy)
                    nc.scalar.activation(kT_st[:, 4:6, :], ps[:, kT_bank(c) + 1, 0:256].rearrange("p (s t) -> p s t", s=2),
                                         ACT.Copy).then_inc(kt_act, 1)
                    if c + 1 < NSC:
                        exp_d(C + 1)
                    if h == 0 and c == NSC - 1:
                        act.wait_ge(s_b, 1)
                        act.wait_ge(on_dve, 4)
                        bs = b_samp[:].rearrange("p s (b t) -> p s b t", b=SB)[:, :, :, ST - 1:ST]
                        nc.scalar.activation(sq_in, b_samp[:], ACT.Exp).then_inc(s_e1, 1)
                        nc.scalar.activation(sk_in, b_samp[:], ACT.Exp, scale=-1.0).then_inc(s_e1, 1)
                        nc.scalar.activation(dsamp.unsqueeze(3), bs, ACT.Exp).then_inc(s_e1, 1)
                        act.wait_ge(s_d, 1)
                        nc.scalar.activation(sk_out, sk_out, ACT.Exp).then_inc(s_e3, 1)
                    if c >= 1:
                        rstd_main(C - 1)
                    copy_o(C)
                    if c == 0:
                        split_hi(u0 + O0_UNIT)
                    if c >= 2:
                        out_hi(C - 2)
                out_hi(C0 + NSC - 2)
                split_hi(u0 + O0_UNIT + 1)
                if h == 0:
                    act.wait_ge(s_t, 1)
                    act.wait_ge(on_dve, 6)
                    nc.scalar.activation(skT[:, 0:4, :], ps[0:NS, 2, :].rearrange("p (s t) -> p s t", s=4), ACT.Copy)
                    nc.scalar.activation(skT[:, 4:6, :], ps[0:NS, 3, 0:256].rearrange("p (s t) -> p s t", s=2),
                                         ACT.Copy).then_inc(s_tc, 1)
                    act.wait_ge(s_o, 1)
                    for g in range(2):
                        so = ps[:, g, 0:4 * NS].rearrange("p (n t) -> p n t", n=4)
                        nc.scalar.activation(s_tiles(g), by_two(so), ACT.Copy).then_inc(s_ocp, 1)
                        nc.scalar.activation(sum_place(0, g, True), so, ACT.Square).then_inc(s_osq, 1)
                rstd_main(C0 + NSC - 1)
                if h == 0:
                    act.wait_ge(s_ss, 1)
                    for g in range(2):
                        rstd(0, g, ps[:, g, 4 * NS:8 * NS].rearrange("p (n t) -> p n t", n=4), g + 1,
                             s_ln, s_rn, NS, True)
                out_hi(C0 + NSC - 1)

                for r in range(O_UNITS):
                    if r:
                        split_hi(u0 + O0_UNIT + r + 1)
                    if r == 0:
                        if h == 0:
                            act.wait_ge(s_og, 1)
                            nc.scalar.activation(pr_att[:, :, 0, :], p_samp[:, 0:NH, :],
                                                 ACT.Copy).then_inc(oh_act, 1)
                        squares(h + 1)
                    for k in turns_at(h, r):
                        if k is not None:
                            turned_hi(h + 1, k)

            def silu(i, st):
                act.wait_ge(step_pe, i * 6 + (st + 1))
                act.wait_ge(gl_done, i * 6 + (st + 1))
                w = FF_CHUNKS[st // 2][1]
                nc.scalar.activation(gated[:, st % 2, 0:w], ps[:, 2 * (st % 2), 0:w], ACT.Silu).then_inc(silu_f, 1)

            def split_w2(i):
                act.wait_ge(raw0_ld, i * 32 + 16 * (F0_UNIT + 2))
                nc.scalar.activation(whi[2][:], raw0[:], ACT.Copy).then_inc(hi_done, 1)

            def split_next(i):
                act.wait_ge(raw0_ld, i * 32 + 16 * (F0_UNIT + 3))
                nc.scalar.activation(whi[0][:], raw0[:], ACT.Copy).then_inc(hi_done, 1)
                act.wait_ge(raw1_ld, i * 16 + 16)
                nc.scalar.activation(whi[1][:], raw1[:], ACT.Copy).then_inc(hi_done, 1)

            def ffn_group(i):
                for st in range(6):
                    silu(i, st)
                    if st == 1:
                        split_w2(i)

            act.wait_ge(raw0_ld, 16 * (F0_UNIT + 1))
            act.wait_ge(used, F0_UNIT)
            nc.scalar.activation(whi[1][:], raw0[:], ACT.Copy).then_inc(hi_done, 1)
            squares(3)
            silu(0, 0)
            for k in range(KT_D):
                turned_hi(3, k)
            split_w2(0)
            for st in range(1, 6):
                silu(0, st)
            split_next(0)
            with act.Fori(1, GROUPS - 1) as i:
                ffn_group(i)
                split_next(i)
            ffn_group(GROUPS - 1)
            act.preload_act_table_set("natural_log_exp_and_others")
            for n, t in enumerate(FINAL_TILES):
                rows = P if t < 8 else NS
                at = OUT_TILES.index(t)
                if n == 6:
                    act.wait_ge(y_dve, (GROUPS - 1) * 18 + 2 * (OUT_TILES.index(8) + 1) + 4)
                    fold(raw1[0:NS, D:2 * D])
                if n < 8:
                    act.wait_ge(y_dve, (GROUPS - 1) * 18 + 2 * (at + 1) + 4)
                if t == 8:
                    act.wait_ge(fold_dve, 2)
                if n:
                    act.wait_ge(sqf, n)
                if n < 8:
                    nc.scalar.activation(raw1[0:rows, 0:D], x_res[0:rows, PLACE[t], :], ACT.Square,
                                         accum_out=ms[0:rows, t:t + 1]).then_inc(sqf, 1)
                    act.wait_ge(sqf, n + 1)
                else:
                    for q, stat in enumerate((ms[:, t:t + 1], ms2)):
                        act.wait_ge(y_dve, (GROUPS - 1) * 18 + 2 * at + q + 5)
                        nc.scalar.activation(raw1[:, 512 * q:512 * (q + 1)],
                                             x_res[:, PLACE[t], 512 * q:512 * (q + 1)], ACT.Square,
                                             accum_out=stat).then_inc(sqf, 1)
                    act.wait_ge(ms_dve, 1)
                inverse_root(ms[0:rows, t:t + 1], rs[0:rows, t:t + 1], lnf, n + 1, rsf)

        @block.vector
        def _(dve):
            def split_lo(u):
                size = L_SIZE if u % HALF_UNITS == L_UNIT else 2048
                s = slot_of(u)
                first = 0
                if u in IN_HALVES:
                    first = 1024
                    dve.wait_ge(half_done, IN_HALVES.index(u) + 1)
                    nc.vector.tensor_tensor(wlo[s][:, 0:first], raw_of(u)[:, 0:first],
                                            whi[s][:, 0:first].bitcast(F32), ALU.subtract)
                dve.wait_ge(hi_done, u + 1)
                nc.vector.tensor_tensor(wlo[s][:, first:size], raw_of(u)[:, first:size],
                                        whi[s][:, first:size].bitcast(F32), ALU.subtract).then_inc(lo_done, 1)

            def scale(n):
                main, samp = stage_parts(n)[:2]
                dve.wait_ge(rs_done, groups_before(n + 1))
                for place, rows, x, scratch in main + ([samp] if samp else []):
                    nc.vector.tensor_scalar(scratch, x, rs[0:rows, place:place + 1], None,
                                            ALU.mult).then_inc(xn_done, 1)

            def first_scale(group):
                dve.wait_ge(rs_done, group + 1)
                for place, rows, x, scratch in first_tiles(group):
                    nc.vector.tensor_scalar(scratch, x, rs[0:rows, place:place + 1], None,
                                            ALU.mult).then_inc(xn_done, 1)

            def first_lo(p, kk):
                dve.wait_ge(th_done, 4 * p + kk + 1)
                for e in range(2):
                    k, cols = 2 * kk + e, slice(256 * p, 256 * (p + 1))
                    last = nc.vector.scalar_tensor_tensor(
                        out=h_lo[:, k, cols], in0=ps[:, 2 * kk + 1, 256 * e:256 * (e + 1)],
                        scalar=pv[:, V_GMIX + k:V_GMIX + k + 1], in1=h_hi[:, k, cols].bitcast(F32),
                        op0=ALU.mult, op1=ALU.subtract)
                last.then_inc(tl_done, 1)

            def turned_lo(n, k):
                main, samp, hi, lo, mcol, scol, gain = stage_parts(n)

                def part(width, src, m, col):
                    return nc.vector.scalar_tensor_tensor(
                        out=lo[:, m, col:col + width], in0=src, scalar=pv[:, gain + m:gain + m + 1],
                        in1=hi[:, m, col:col + width].bitcast(F32), op0=ALU.mult, op1=ALU.subtract)

                dve.wait_ge(th_done, turns_before(n) + k + 1)
                bank = turn_bank(n, k)
                if n == 2 and k == 0:
                    dve.wait_ge(out_st, 2 * 16 * NH)
                if k < KT_D:
                    last = part(HALF, ps[:, bank, :], k, mcol)
                else:
                    for m in range(KT_D):
                        last = part(NS, ps[:, bank, m * NS:(m + 1) * NS], m, scol)
                last.then_inc(tl_done, 1)

            def fold(count, scratch):
                dve.wait_ge(fold_act, count)
                nc.vector.tensor_tensor(x_res[0:NS, 8, :], x_res[0:NS, 8, :], scratch, ALU.add).then_inc(fold_dve, 1)

            def out_lo(C):
                c = C % NSC
                dve.wait_ge(oh_act, split_count(C))
                nc.vector.tensor_tensor(pr_main[:, c, 0:NH, :], p_main[:, c, 0:NH, :],
                                        pr_main[:, c, GT:GT + NH, :].bitcast(F32), ALU.subtract).then_inc(ol_dve, 1)

            def s_mask(m):
                slot, b0, _ = piece(m)
                if m >= 2:
                    dve.wait_ge(s_kv, m - 1)
                nc.vector.tensor_tensor(
                    skm[m % 2], skT[:, slot, :].unsqueeze(1).broadcast_to((NS, 4, P)),
                    bmask[:, b0:b0 + 4].unsqueeze(2).broadcast_to((NS, 4, P)), ALU.mult).then_inc(s_dm, 1)

            def s_update(m):
                slot, b0, bank = piece(m)
                dve.wait_ge(s_kv, m + 1)
                for b in range(4):
                    st = s_state[:, slot, b0 + b, :]
                    last = nc.vector.scalar_tensor_tensor(
                        out=st, in0=st, scalar=dsamp[:, slot, b0 + b:b0 + b + 1],
                        in1=ps[:, bank, b * V:(b + 1) * V], op0=ALU.mult, op1=ALU.add)
                last.then_inc(s_upd, 1)

            def d_of(C):
                c, j = C % NSC, C % 2
                if c == 0:
                    dve.wait_ge(h_lo_used, C // NSC + 1)
                else:
                    dve.wait_ge(used, HALF_UNITS * (C // NSC) + O0_UNIT)
                dve.wait_ge(b_done, C + 1)
                if C >= 2:
                    dve.wait_ge(att_pe, 2 * (C - 1))
                    dve.wait_ge(pool_k, C - 1)
                b = b_main[:, c].rearrange("p s (c t) -> p (s c) t", t=CH)
                nc.vector.tensor_tensor(k_out[j][:].rearrange("p s (c t) -> p (s c) t", t=CH),
                                        b[:, :, CH - 1:CH].broadcast_to((P, SLOTS * NCH, CH)), b,
                                        ALU.subtract).then_inc(d_done, 1)

            def prep(C):
                c, j = C % NSC, C % 2
                q, k = p_main[:, c, QT:QT + SLOTS, :], p_main[:, c, KTL:KTL + SLOTS, :]
                dve.wait_ge(e1_done, 3 * (C + 1))
                nc.vector.tensor_tensor(q_in[j][:], q_in[j][:], q, ALU.mult)
                nc.vector.tensor_tensor(k_in[j][:], k_in[j][:], k, ALU.mult)
                dve.wait_ge(e3_done, C + 1)
                nc.vector.tensor_tensor(k_out[j][:], k_out[j][:], k, ALU.mult).then_inc(prep1_done, 1)
                dve.wait_ge(prep1_done, C + 1)
                dve.wait_ge(fac_a, C + 1)

                def chunks(buf, first):
                    return buf[:, :, first:first + 64].rearrange("p s (c t) -> p s c t", c=2)

                nc.vector.tensor_tensor(chunks(q_64[j], 0), chunks(q_in[j], 64),
                                        f64[j].unsqueeze(3).broadcast_to((P, SLOTS, 2, CH)), ALU.mult)
                nc.vector.tensor_tensor(chunks(k_64[j], 0), chunks(k_out[j], 0),
                                        g64[j].unsqueeze(3).broadcast_to((P, SLOTS, 2, CH)),
                                        ALU.mult).then_inc(prep_done, 1)

            def mask(C):
                for g in range(2):
                    dve.wait_ge(att_pe, 2 * C + g + 1)
                    dve.wait_ge(zero_att, C // NSC + 1)
                    if C >= 1:
                        dve.wait_ge(o_pe, 2 * (C - 1) + g + 1)
                    nc.vector.copy_predicated(att[:, g], causal.unsqueeze(1).broadcast_to((P, 4, SC)),
                                              ps[:, g, :].rearrange("p (n t) -> p n t", n=4)).then_inc(att_dve, 1)

            def norm_o(C):
                c = C % NSC
                for g in range(2):
                    dve.wait_ge(rn_act, 2 * C + g + 1)
                    o = p_main[:, c, 4 * g:4 * g + 4, :]
                    nc.vector.tensor_tensor(o, o, sum_place(C, g), ALU.mult).then_inc(on_dve, 1)

            def update_state(C):
                j = C % 2
                dve.wait_ge(kv_pe, C + 1)
                dve.wait_ge(o_pe, 2 * (C + 1))
                dve.wait_ge(fac_b, C + 1)
                if C == 0:
                    dve.wait_ge(zero_state, 1)
                else:
                    dve.wait_ge(st_done, C)
                for slot in range(SLOTS):
                    bank, at = (4, slot) if slot < 4 else (5, slot - 4)
                    last = nc.vector.scalar_tensor_tensor(
                        out=state[:, slot, :], in0=state[:, slot, :], scalar=dtot[j][:, slot, :],
                        in1=ps[:, bank, at * V:(at + 1) * V], op0=ALU.mult, op1=ALU.add)
                last.then_inc(st_done, 1)

            nc.vector.memset(val[NS:P, 4, :], 0.0)
            nc.vector.memset(x_res[NS:P, 8, :], 0.0)
            dve.sem_inc(ev_v, 2)
            for h in range(2):
                u0 = HALF_UNITS * h
                bc = (h == 0)

                def evacuate(i, e):
                    u = u0 + e
                    dve.wait_ge(used, i * 2 + (u + 1))
                    b0 = 4 * (u % 2) + 2
                    tile = i * 4 + (2 * e + 1)
                    for q in range(2):
                        src = ps[:, b0 + q, 0:256].rearrange("p (c o t) -> p c o t", c=2, o=1)
                        last = nc.vector.tensor_copy(p_main[:, 2 * q:2 * q + 2, bass.ds(tile, 1), :], src)
                    if bc:
                        last = nc.vector.tensor_copy(p_samp[:, bass.ds(tile, 1), :],
                                                     ps[:, b0 + 1, 256:256 + NS].unsqueeze(1))
                    last.then_inc(ev_v, 1)

                if h == 0:
                    first_scale(0)
                    split_lo(0)
                    for kk in range(4):
                        first_lo(0, kk)
                    first_scale(1)
                    split_lo(1)
                    first_scale(2)
                    for kk in range(4):
                        first_lo(1, kk)
                    turned_lo(0, KT_D)
                    dve.wait_ge(pv_ld, 16)
                    lbp = pv[:, V_LB:V_LB + 8].rearrange("p (a n) -> p a n", a=2)
                    nc.vector.tensor_tensor(lbw[:, 2, :], lbp[:, 0, :], lbp[:, 1, :], ALU.max).then_inc(zm_done, 1)
                    dve.wait_ge(zm_done, 1)
                    nc.vector.tensor_tensor(lbw[:, 0:2, :], lbp, lbw[:, 2:3, :].broadcast_to((P, 2, HB)),
                                            ALU.subtract).then_inc(lb_v, 1)
                    evacuate(0, 0)
                    split_lo(2)
                    dve.wait_ge(lb_e, 1)
                    nc.vector.tensor_tensor(lbw[:, 2, :], lbw[:, 0, :], lbw[:, 1, :], ALU.add).then_inc(lb_v, 1)
                    dve.wait_ge(lb_v, 2)
                    nc.vector.reciprocal(lbw[:, 2, :], lbw[:, 2, :]).then_inc(lb_v, 1)
                    dve.wait_ge(lb_v, 3)
                    nc.vector.tensor_tensor(lb, lbw[:, 0, :], lbw[:, 2, :], ALU.mult).then_inc(lb_v, 1)
                    dve.wait_ge(lb_v, 4)
                    nc.vector.tensor_scalar(omlb, lb, -1.0, 1.0, ALU.mult, ALU.add).then_inc(lb_v, 1)
                    dve.wait_ge(lb_v, 5)
                    evacuate(0, 1)
                else:
                    fold(1, val[0:NS, 4, :])
                    nc.vector.memset(x_res[NS:P, 8, :], 0.0)
                with dve.Fori(1 - h, A_UNITS // 2) as i:
                    for e in range(2):
                        u = u0 + e
                        s = slot_of(u + 1)
                        dve.wait_ge(hi_done, i * 2 + (u + 2))
                        nc.vector.tensor_tensor(wlo[s][:], raw0[:], whi[s][:].bitcast(F32),
                                                ALU.subtract).then_inc(lo_done, 1)
                        evacuate(i, e)
                u = u0 + L_UNIT
                split_lo(u + 1)
                dve.wait_ge(used, u + 1)
                w = 256 + half(h)
                nc.vector.tensor_copy(lr_t[h][:, 256:256 + w], ps[0:RANK2, 4 * (u % 2) + 1, 0:w]).then_inc(ev_v, 1)

                def values(v):
                    u = u0 + V0_UNIT + v
                    if v < 2:
                        split_lo(u + 1)
                    dve.wait_ge(used, u + 1)
                    for t in range(2, 5 if bc else 4):
                        rows = P if t < 4 else NS
                        last = nc.vector.tensor_copy(
                            val[0:rows, t, 256 * v:256 * (v + 1)],
                            ps[0:rows, 4 * (u % 2) + t // 2, 256 * (t % 2):256 * (t % 2 + 1)])
                    last.then_inc(ev_v, 1)

                values(0)
                for p in range(2):
                    dve.wait_ge(z_pe, 2 * h + p + 1)
                    last = nc.vector.tensor_scalar(
                        b_main[:, :, p, :], ps[:, 3 + 4 * p, :].rearrange("p (c t) -> p c t", c=NSC),
                        pv[:, V_BA + p:V_BA + p + 1], None, ALU.add)
                last.then_inc(z_dve, 1)
                dve.wait_ge(sig_done, 2 if h == 0 else 3)
                for n in range(HB):
                    fs = [p_main[:, :, FT + n, :]] + ([p_samp[:, FT + n, :]] if bc else [])
                    for f in fs:
                        last = nc.vector.tensor_scalar(f, f, omlb[:, n:n + 1], lb[:, n:n + 1], ALU.mult, ALU.add)
                last.then_inc(f_done, 1)
                values(1)
                if bc:
                    dve.wait_ge(z_s_pe, 1)
                    for p in range(2):
                        last = nc.vector.tensor_scalar(b_samp[:, p, :], ps[:, 3, p * NS:(p + 1) * NS],
                                                       pv[:, V_BA + p:V_BA + p + 1], None, ALU.add)
                    last.then_inc(z_s_dve, 1)
                split_lo(u0 + V0_UNIT + 3)
                dve.wait_ge(azl_done, 2 if h == 0 else 3)
                zs = [(b_main[:, :, 0:2, :], az_m)] + ([(b_samp[:, 0:2, :], az_s)] if bc else [])
                for z, l in zs:
                    last = nc.vector.scalar_tensor_tensor(out=z, in0=z, scalar=0.0, in1=l, op0=ALU.min,
                                                          op1=ALU.subtract)
                last.then_inc(la_done, 1)
                dve.wait_ge(la_done, h + 1)
                for z, _ in zs:
                    last = nc.vector.tensor_scalar(z, z, 1.0 / GATE_NORM, None, ALU.mult)
                last.then_inc(la2_done, 1)
                dve.wait_ge(la2_done, h + 1)

                def cumsum(c):
                    if c < NSC:
                        b = b_main[:, c].rearrange("p s t -> p (s t)")
                        nc.vector.tensor_tensor_scan(b, m32, b, 0.0, ALU.mult, ALU.add).then_inc(b_done, 1)
                    else:
                        b = b_samp[:].rearrange("p s t -> p (s t)")
                        nc.vector.tensor_tensor_scan(b, m8, b, 0.0, ALU.mult, ALU.add).then_inc(s_b, 1)

                dve.wait_ge(c_ld, 48)
                dve.wait_ge(lnf_done, 2 if h == 0 else 3)
                cumsum(0)
                dve.wait_ge(lnf_done, 2 if h == 0 else 3)
                ks = [p_main[:, :, FT:FT + HB, :]] + ([p_samp[:, FT:FT + HB, :]] if bc else [])
                for k in ks:
                    last = nc.vector.tensor_scalar(k, k, -1.0, 1.0, ALU.mult, ALU.add)
                last.then_inc(k_done, 1)
                values(2)

                dve.wait_ge(qs_done, h + 1)
                dve.wait_ge(k_done, h + 1)
                C0 = NSC * h
                d_of(C0)
                prep(C0)
                cumsum(1)
                values(3)
                for c in range(NSC):
                    C = C0 + c
                    sample = (h == 0 and c == NSC - 1)
                    if c + 1 < NSC:
                        d_of(C + 1)
                    if sample:
                        dve.wait_ge(s_b, 1)
                        dve.wait_ge(on_dve, 4)
                        b = b_samp[:].rearrange("p s (b t) -> p (s b) t", t=ST)
                        nc.vector.tensor_tensor(sk_out.rearrange("p s (b t) -> p (s b) t", t=ST),
                                                b[:, :, ST - 1:ST].broadcast_to((P, SLOTS * SB, ST)), b,
                                                ALU.subtract).then_inc(s_d, 1)
                    mask(C)
                    if c + 1 < NSC:
                        prep(C + 1)
                    if sample:
                        dve.wait_ge(s_e1, 3)
                        nc.vector.tensor_tensor(sq_in, sq_in, p_samp[:, QT:QT + SLOTS, :], ALU.mult)
                        nc.vector.tensor_tensor(sk_in, sk_in, p_samp[:, KTL:KTL + SLOTS, :],
                                                ALU.mult).then_inc(s_q, 1)
                        dve.wait_ge(s_e3, 1)
                        nc.vector.tensor_tensor(sk_out, sk_out, p_samp[:, KTL:KTL + SLOTS, :],
                                                ALU.mult).then_inc(s_prep, 1)
                        dve.wait_ge(s_q, 1)
                        dve.wait_ge(s_zero, 1)
                        for e in range(2):
                            rows = slice(KA * e, KA * (e + 1))
                            last = nc.vector.tensor_copy(
                                sq_pair[rows, :, :, e, :],
                                sq_in[rows, 0:HA // 2, :].rearrange("p s (b t) -> p s b t", b=SB))
                        last.then_inc(s_pair, 1)
                    if c >= 1:
                        norm_o(C - 1)
                    if sample:
                        dve.wait_ge(s_att_pe, 1)
                        dve.wait_ge(s_zero, 1)
                        for g in range(2):
                            last = nc.vector.copy_predicated(
                                s_att[0:NS, 4 * g:4 * g + 4, :], smask.unsqueeze(1).broadcast_to((NS, 4, NS)),
                                ps[0:NS, g, 0:4 * NS].rearrange("p (n t) -> p n t", n=4))
                        last.then_inc(s_att_dve, 1)
                    update_state(C)
                    if c == 0:
                        cumsum(2)
                        split_lo(u0 + O0_UNIT)
                    if c == 1:
                        cumsum(3)
                        if bc:
                            cumsum(NSC)
                    if c >= 2:
                        out_lo(C - 2)
                dve.wait_ge(o_act, 2 * (C0 + NSC))
                dve.wait_ge(g_done, h + 1)
                o = p_main[:, NSC - 1, 0:NH, :]
                nc.vector.tensor_tensor(o, o, p_main[:, NSC - 1, GT:GT + NH, :], ALU.mult).then_inc(og_dve, 1)
                out_lo(C0 + NSC - 2)
                split_lo(u0 + O0_UNIT + 1)
                if h == 0:
                    dve.wait_ge(s_tc, 1)
                    dve.wait_ge(on_dve, 6)
                    s_mask(0)
                    s_mask(1)
                dve.wait_ge(og_dve, h + 1)
                norm_o(C0 + NSC - 1)

                m = 0
                for r in range(O_UNITS):
                    u = u0 + O0_UNIT + r
                    if r:
                        split_lo(u + 1)
                    if h == 1 and r == 0:
                        out_lo(C0 + NSC - 1)
                        scale(2)
                    if h == 0 and r < 2:
                        for t in range(5):
                            if r == 0 and t == 2:
                                dve.wait_ge(s_rn, 2)
                                for g in range(2):
                                    o = s_tiles(g)
                                    last = nc.vector.tensor_tensor(o, o, by_two(sum_place(0, g, True)), ALU.mult)
                                last.then_inc(s_on, 1)
                                out_lo(C0 + NSC - 1)
                            if r == 0 and t == 3:
                                dve.wait_ge(oh_act, NSC + 1)
                                nc.vector.tensor_tensor(pr_att[:, :, 1, :], p_samp[:, 0:NH, :],
                                                        pr_att[:, :, 0, :].bitcast(F32),
                                                        ALU.subtract).then_inc(ol_dve, 1)
                            for _ in range(S_PIECES[r][t]):
                                s_update(m)
                                if m + 2 < 2 * SLOTS:
                                    s_mask(m + 2)
                                m += 1
                    if h == 0 and r == 1:
                        scale(1)
                    for k in turns_at(h, r):
                        if k is not None:
                            turned_lo(h + 1, k)
                    dve.wait_ge(used, u + 1)
                    if h == 1 and r == 0:
                        dve.wait_ge(xr_ld, 16 * 8)
                    cols = slice(256 * r, 256 * (r + 1))
                    order = [2, 3, 4, 0, 1] if h == 0 else range(4)
                    for t in order:
                        if h == 0 and r == 0 and t in (2, 0):
                            dve.wait_ge(xr_ld, 32 if t == 2 else 64)
                        x = x_res[:, half_tiles(h)[t][0], cols]
                        last = nc.vector.tensor_tensor(
                            x, ps[:, 4 * (u % 2) + t // 2, 256 * (t % 2):256 * (t % 2 + 1)], x, ALU.add)
                    last.then_inc(ev_v, 1)

            def lo_of(slot, raw, count):
                dve.wait_ge(hi_done, count)
                nc.vector.tensor_tensor(wlo[slot][:], raw[:], whi[slot][:].bitcast(F32),
                                        ALU.subtract).then_inc(lo_done, 1)

            dve.sem_inc(gl_done, 2)
            dve.sem_inc(y_dve, 4)

            def gate_step(i, st):
                ch, ft = divmod(st, 2)
                col, w = FF_CHUNKS[ch]
                n, s = i * 6 + (st + 1), st % 2
                dve.wait_ge(silu_f, n)
                nc.vector.tensor_tensor(gated[:, s, 0:w], gated[:, s, 0:w], ps[:, 2 * s + 1, 0:w],
                                        ALU.mult).then_inc(gm_done, 1)
                dve.wait_ge(gm_done, n)
                main = min(w, SEQ - col)
                parts = [(gated[:, s, 0:main], g_hi[:, ft, col:col + main], g_lo[:, ft, col:col + main])]
                if main < w:
                    parts.append((gated[:, s, main:w], g_samp[:, ft, 0], g_samp[:, ft, 1]))
                for g, hi, lo in parts:
                    last = nc.vector.tensor_copy(hi, g)
                last.then_inc(gh_done, 1)
                dve.wait_ge(gh_done, n)
                for g, hi, lo in parts:
                    last = nc.vector.tensor_tensor(lo, g, hi.bitcast(F32), ALU.subtract)
                last.then_inc(gl_done, 1)

            def final_norm(n):
                t = FINAL_TILES[n]
                rows = P if t < 8 else NS
                dve.wait_ge(rsf, n + 1)
                for a, b in ([(0, D)] if n < 8 else [(0, 512), (512, D)]):
                    x = x_res[0:rows, PLACE[t], a:b]
                    nc.vector.scalar_tensor_tensor(out=x, in0=x, scalar=rs[0:rows, t:t + 1], in1=nf[0:rows, a:b],
                                                   op0=ALU.mult, op1=ALU.mult).then_inc(yf_done, 1)

            def add_outputs(i, last_group):
                for n, t in enumerate(OUT_TILES):
                    for q in range(2):
                        m = 2 * n + q
                        dve.wait_ge(y_pe, i * 18 + (m + 1))
                        x = x_res[:, PLACE[t], 512 * q:512 * (q + 1)]
                        nc.vector.tensor_tensor(x, ps[:, 4 + m % 4, :], x, ALU.add).then_inc(y_dve, 1)
                        if last_group and n == 8 and q == 0:
                            final_norm(6)
                    if not last_group and n == 2:
                        lo_of(0, raw0, i * 3 + (F0_UNIT + 4))
                    if not last_group and n == 5:
                        lo_of(1, raw1, i * 3 + (F0_UNIT + 5))
                    if last_group and 1 <= n <= 6:
                        final_norm(n - 1)
                    if last_group and n == 7:
                        fold(2, raw1[0:NS, D:2 * D])
                    if last_group and n == 8:
                        final_norm(7)
                        dve.wait_ge(sqf, 10)
                        nc.vector.tensor_tensor(ms[:, 7:8], ms[:, 7:8], ms2, ALU.add).then_inc(ms_dve, 1)
                        final_norm(8)

            def ffn_group(i, last_group):
                for st in range(6):
                    gate_step(i, st)
                    if st == 1:
                        lo_of(2, raw0, i * 3 + (F0_UNIT + 3))
                add_outputs(i, last_group)

            lo_of(1, raw0, F0_UNIT + 2)
            scale(3)
            gate_step(0, 0)
            for k in range(KT_D):
                turned_lo(3, k)
            lo_of(2, raw0, F0_UNIT + 3)
            for st in range(1, 6):
                gate_step(0, st)
            add_outputs(0, False)
            with dve.Fori(1, GROUPS - 1) as i:
                ffn_group(i, False)
            dve.wait_ge(nf_ld, 16)
            ffn_group(GROUPS - 1, True)

        @block.tensor
        def _(pe):
            def three(out, a_hi, a_lo, b_hi, b_lo, first, last):
                nc.tensor.matmul(out, a_hi, b_hi, start=first, stop=False)
                nc.tensor.matmul(out, a_hi, b_lo, start=False, stop=False)
                return nc.tensor.matmul(out, a_lo, b_hi, start=False, stop=last)

            def both(out, a, b_hi, b_lo, first, last):
                nc.tensor.matmul(out, a, b_hi, start=first, stop=False)
                return nc.tensor.matmul(out, a, b_lo, start=False, stop=last)

            def first_turn(p, kk):
                pe.wait_ge(xn_done, 2 * p + 2)
                if p:
                    pe.wait_ge(tl_done, kk + 1)
                for e in range(2):
                    k = 2 * kk + e
                    for j, (_, _, _, scratch) in enumerate(first_tiles(p)):
                        last = nc.tensor.transpose(ps[:, 2 * kk + 1, 256 * e + j * P:256 * e + (j + 1) * P],
                                                   scratch[:, k // 4, (k % 4) * P:(k % 4 + 1) * P], ident)
                last.then_inc(tr_done, 1)

            def turn(n, k):
                main, samp = stage_parts(n)[:2]
                t0, bank = turns_before(n), turn_bank(n, k)
                if k == 0:
                    pe.wait_ge(xn_done, tiles_before(n) + 4)
                if k == KT_D:
                    pe.wait_ge(xn_done, tiles_before(n + 1))
                ring = {1: 2, 2: 2, 3: 4}.get(n)
                if n == 0:
                    pe.wait_ge(tl_done, 5)
                elif k >= ring:
                    pe.wait_ge(tl_done, t0 + k - ring + 1)
                if k < KT_D:
                    for j, (_, _, _, scratch) in enumerate(main):
                        last = nc.tensor.transpose(ps[:, bank, j * P:(j + 1) * P],
                                                   scratch[:, k // 4, (k % 4) * P:(k % 4 + 1) * P], ident)
                else:
                    for m in range(KT_D):
                        last = nc.tensor.transpose(ps[:, bank, m * NS:(m + 1) * NS],
                                                   samp[3][:, m // 4, (m % 4) * P:(m % 4 + 1) * P], ident[0:NS, 0:NS])
                last.then_inc(tr_done, 1)

            pe.wait_ge(id_ld, 16)
            for h in range(2):
                u0 = HALF_UNITS * h
                chunks = [(0, 256), (256, 256 + half(h))]

                def a_chunk(u, q, signal, tiles=(0, 1)):
                    s = slot_of(u)
                    w_hi = whi[s][:].rearrange("p (k n) -> p k n", k=KT_D)
                    w_lo = wlo[s][:].rearrange("p (k n) -> p k n", k=KT_D)
                    col, w = chunks[q]
                    for ft in tiles:
                        for k in range(KT_D):
                            a, b = slice(ft * P, (ft + 1) * P), slice(col, col + w)
                            last = three(ps[:, 4 * (u % 2) + 2 * ft + q, 0:w],
                                         w_hi[:, k, a], w_lo[:, k, a], h_hi[:, k, b], h_lo[:, k, b],
                                         k == 0, k == KT_D - 1)
                    if signal:
                        last.then_inc(used, 1)

                if h == 0:
                    for kk in range(4):
                        first_turn(0, kk)
                    w_hi = whi[0][:].rearrange("p (k n) -> p k n", k=KT_D)
                    w_lo = wlo[0][:].rearrange("p (k n) -> p k n", k=KT_D)
                    for m, (w, x) in enumerate(((w_hi, h_hi), (w_lo, h_hi), (w_hi, h_lo))):
                        if m == 0:
                            pe.wait_ge(hi_done, 1)
                        if m == 1:
                            pe.wait_ge(lo_done, 1)
                        for ft in range(2):
                            for k in range(KT_D):
                                if m != 1 and ft == 0 and k % 2 == 0:
                                    pe.wait_ge(tl_done if m else th_done, k // 2 + 1)
                                nc.tensor.matmul(ps[:, 2 * ft, 0:256], w[:, k, ft * P:(ft + 1) * P], x[:, k, 0:256],
                                                 start=(m == 0 and k == 0), stop=(m == 2 and k == KT_D - 1))
                    for kk in range(4):
                        first_turn(1, kk)
                    pe.wait_ge(lo_done, 2)
                    a_chunk(1, 0, False, (0,))
                    turn(0, KT_D)
                    a_chunk(1, 0, False, (1,))
                    pe.wait_ge(tl_done, turns_before(1))
                    a_chunk(0, 1, True)
                    a_chunk(1, 1, True)
                else:
                    pe.wait_ge(tl_done, turns_before(2))
                with pe.Fori(1 - h, A_UNITS // 2) as i:
                    for e in range(2):
                        u = u0 + e
                        pe.wait_ge(lo_done, i * 2 + (u + 1))
                        pe.wait_ge(ev_v, i * 2 + (u + 1))
                        pe.wait_ge(ev_a, i * 2 + (O0_UNIT * h + e + 1))
                        s = slot_of(u)
                        w_hi = whi[s][:].rearrange("p (k n) -> p k n", k=KT_D)
                        w_lo = wlo[s][:].rearrange("p (k n) -> p k n", k=KT_D)
                        for ft in range(2):
                            for q, (col, w) in enumerate(chunks):
                                for k in range(KT_D):
                                    a, b = slice(ft * P, (ft + 1) * P), slice(col, col + w)
                                    last = three(ps[:, 4 * (u % 2) + 2 * ft + q, 0:w],
                                                 w_hi[:, k, a], w_lo[:, k, a], h_hi[:, k, b], h_lo[:, k, b],
                                                 k == 0, k == KT_D - 1)
                        last.then_inc(used, 1)
                u = u0 + L_UNIT
                s = slot_of(u)
                pe.wait_ge(lo_done, u + 1)
                pe.wait_ge(ev_v, u + 1)
                pe.wait_ge(ev_a, 2 + act_copies_before(u - 1))
                pe.wait_ge(paired, h + 1)
                w = whi[s][:, 0:L_SIZE].rearrange("p (k n) -> p k n", k=KT_D)
                for q, (col, width) in enumerate(chunks):
                    for k in range(KT_D):
                        last = both(ps[0:RANK2, 4 * (u % 2) + q, 0:width], w[:, k], h_hi[:, k, col:col + width],
                                    h_lo[:, k, col:col + width], k == 0, k == KT_D - 1)
                last.then_inc(used, 1)

                def token_major(r):
                    u = u0 + r
                    s = slot_of(u)
                    pe.wait_ge(lo_done, u + 1)
                    pe.wait_ge(ev_v, u + 1)
                    pe.wait_ge(ev_a, 2 + act_copies_before(u - 1))
                    w_hi = whi[s][:].rearrange("p (k n) -> p k n", k=KT_D)
                    w_lo = wlo[s][:].rearrange("p (k n) -> p k n", k=KT_D)
                    for t, (_, rows, col) in enumerate(half_tiles(h)):
                        for k in range(KT_D):
                            a = slice(col, col + rows)
                            last = three(ps[0:rows, 4 * (u % 2) + t // 2, 256 * (t % 2):256 * (t % 2 + 1)],
                                         h_hi[:, k, a], h_lo[:, k, a], w_hi[:, k], w_lo[:, k],
                                         k == 0, k == KT_D - 1)
                    last.then_inc(used, 1)

                token_major(V0_UNIT)
                pe.wait_ge(ev_a, 2 + act_copies_before(u0 + V0_UNIT))
                pe.wait_ge(ev_v, u0 + V0_UNIT + 2)
                if h == 0:
                    pe.wait_ge(c_ld, 48)
                for p in range(2):
                    nc.tensor.matmul(ps[:, 3 + 4 * p, :], wa2[:, p * P:(p + 1) * P], lr_t[h][:, 0:HALF],
                                     start=True, stop=True).then_inc(z_pe, 1)
                token_major(V0_UNIT + 1)
                if h == 0:
                    pe.wait_ge(z_dve, 1)
                    for p in range(2):
                        last = nc.tensor.matmul(ps[:, 3, p * NS:(p + 1) * NS], wa2[:, p * P:(p + 1) * P],
                                                lr_t[0][:, HALF:HALF + NS], start=True, stop=True)
                    last.then_inc(z_s_pe, 1)
                token_major(V0_UNIT + 2)
                u = u0 + V0_UNIT + 3
                s = slot_of(u)
                pe.wait_ge(lo_done, u + 1)
                pe.wait_ge(ev_v, u + 1)
                pe.wait_ge(ev_a, 2 + act_copies_before(u - 1))
                w_hi = whi[s][:].rearrange("p (k n) -> p k n", k=KT_D)
                w_lo = wlo[s][:].rearrange("p (k n) -> p k n", k=KT_D)
                for low in (True, False):
                    for t, (_, rows, col) in enumerate(half_tiles(h)):
                        o = ps[0:rows, 4 * (u % 2) + t // 2, 256 * (t % 2):256 * (t % 2 + 1)]
                        a = slice(col, col + rows)
                        for k in range(KT_D):
                            if low:
                                last = nc.tensor.matmul(o, h_lo[:, k, a], w_hi[:, k],
                                                        start=(k == 0 and t % 2 == 0), stop=False)
                            else:
                                nc.tensor.matmul(o, h_hi[:, k, a], w_hi[:, k], start=False, stop=False)
                                last = nc.tensor.matmul(o, h_hi[:, k, a], w_lo[:, k], start=False,
                                                        stop=(k == KT_D - 1 and (t % 2 == 1 or t == 4)))
                    last.then_inc(h_lo_used if low else used, 1)

                def sums(C):
                    for g in range(2):
                        pe.wait_ge(osq_act, 2 * C + g + 1)
                        nc.tensor.matmul(ps[:, 2 + g, :].rearrange("p (n t) -> p n t", n=4), ones,
                                         sum_place(C, g), start=True, stop=True).then_inc(ss_pe, 1)

                C0 = NSC * h
                for c in range(NSC):
                    C = C0 + c
                    j = C % 2
                    pe.wait_ge(pool_k, C + 1)
                    if c >= 2:
                        pe.wait_ge(ln_act, 2 * (C - 1))
                    for slot in range(SLOTS):
                        bank, at = (kT_bank(c), slot) if slot < 4 else (kT_bank(c) + 1, slot - 4)
                        last = nc.tensor.transpose(ps[:, bank, at * P:(at + 1) * P], k_st[:, slot, :], ident)
                    last.then_inc(kt_pe, 1)
                    if c == 0:
                        pe.wait_ge(ev_a, 2 + act_copies_before(u0 + O0_UNIT))
                        pe.wait_ge(ev_v, u0 + O0_UNIT + 2)
                    pe.wait_ge(prep_done, C + 1)
                    for g in range(2):
                        if C >= 1:
                            pe.wait_ge(att_dve, 2 * (C - 1) + g + 1)
                        for at, n in enumerate(ORDER[4 * g:4 * g + 4]):
                            slot, lo, kw = head_place(n)
                            r, o = slice(lo, lo + kw), at * SC
                            nc.tensor.matmul(ps[:, g, o:o + SC], k_in[j][r, slot, :], q_in[j][r, slot, :],
                                             start=True, stop=True)
                            for a in (0, 64):
                                nc.tensor.matmul(ps[a:a + 32, g, o + a + 32:o + a + 64], k_out[j][r, slot, a:a + 32],
                                                 q_in[j][r, slot, a + 32:a + 64], start=True, stop=True)
                            last = nc.tensor.matmul(ps[0:64, g, o + 64:o + SC], k_64[j][r, slot, :],
                                                    q_64[j][r, slot, :], start=True, stop=True)
                        last.then_inc(att_pe, 1)
                    pe.wait_ge(kt_act, C + 1)
                    if C >= 1:
                        pe.wait_ge(st_done, C)
                    for n in range(NH):
                        slot, lo, kw = head_place(n)
                        bank, at = (4, slot) if slot < 4 else (5, slot - 4)
                        last = nc.tensor.matmul(ps[lo:lo + kw, bank, at * V:(at + 1) * V], kT_st[:, slot, lo:lo + kw],
                                                val[:, c, n * V:(n + 1) * V], start=True, stop=True)
                    last.then_inc(kv_pe, 1)
                    if c >= 1:
                        sums(C - 1)
                    if h == 0 and c == NSC - 1:
                        pe.wait_ge(s_prep, 1)
                        pe.wait_ge(att_dve, 2 * NSC)
                        for m, n in enumerate(ORDER):
                            slot, lo, kw = head_place(n)
                            last = nc.tensor.matmul(ps[0:NS, m // 4, (m % 4) * NS:(m % 4 + 1) * NS],
                                                    sk_in[lo:lo + kw, slot, :], sq_in[lo:lo + kw, slot, :],
                                                    start=True, stop=True)
                        last.then_inc(s_att_pe, 1)
                    pe.wait_ge(pool_q, C + 1)
                    if C == 0:
                        pe.wait_ge(zero_state, 1)
                    for g in range(2):
                        pe.wait_ge(att_dve, 2 * C + g + 1)
                        if C >= 1:
                            pe.wait_ge(osq_act, 2 * (C - 1) + g + 1)
                        for at, n in enumerate(ORDER[4 * g:4 * g + 4]):
                            slot, lo, kw = head_place(n)
                            o = ps[:, 6 + g, at * SC:(at + 1) * SC]
                            nc.tensor.matmul(o, state[lo:lo + kw, slot, :], q_st[j][lo:lo + kw, slot, :],
                                             start=True, stop=False)
                            last = nc.tensor.matmul(o, val[:, c, n * V:(n + 1) * V], att[:, g, at, :],
                                                    start=False, stop=True)
                        last.then_inc(o_pe, 1)
                if h == 0:
                    pe.wait_ge(ln_act, 2 * (NSC - 1))
                    for slot in range(SLOTS):
                        bank, at = (2, slot) if slot < 4 else (3, slot - 4)
                        last = nc.tensor.transpose(ps[0:NS, bank, at * P:(at + 1) * P], sk_out[:, slot, :], ident)
                    last.then_inc(s_t, 1)
                    pe.wait_ge(s_att_dve, 1)
                    pe.wait_ge(st_ld, 16 * NH)
                    pe.wait_ge(s_pair, 1)
                    for p in range(HA // 2):
                        pair = ps[:, 0, 0:4 * NS].rearrange("p (e m t) -> p m e t", e=2, m=2)[:, p]
                        for e in range(2):
                            n = 2 * p + e
                            nc.tensor.matmul(pair[:, e], val[:, 4, n * V:(n + 1) * V], s_att[:, ORDER.index(n), :],
                                             start=(e == 0), stop=False)
                        for b in range(SB):
                            last = nc.tensor.matmul(pair[:, :, b * ST:(b + 1) * ST], s_state[:, p, b, :],
                                                    sq_pair[:, p, b], start=False, stop=(b == SB - 1))
                    for m, n in enumerate(S_PLACES[1]):
                        slot = head_place(n)[0]
                        o = m * NS
                        nc.tensor.matmul(ps[:, 1, o:o + NS], val[:, 4, n * V:(n + 1) * V],
                                         s_att[:, ORDER.index(n), :], start=True, stop=False)
                        for b in range(SB):
                            last = nc.tensor.matmul(ps[:, 1, o + b * ST:o + (b + 1) * ST],
                                                    s_state[:, slot, b, :], sq_in[:, slot, b * ST:(b + 1) * ST],
                                                    start=False, stop=(b == SB - 1))
                    last.then_inc(s_o, 1)
                    pe.wait_ge(s_tc, 1)
                pe.wait_ge(ln_act, 2 * (C0 + NSC - 1))
                sums(C0 + NSC - 1)

                m = 0

                def sample_piece(m):
                    slot, b0, bank = piece(m)
                    pe.wait_ge(s_dm, m + 1)
                    if m == 0:
                        pe.wait_ge(osq_act, 2 * NSC)
                    elif m == 1:
                        pe.wait_ge(ln_act, 2 * NSC)
                    else:
                        pe.wait_ge(s_upd, m - 1)
                    for n in range(NH):
                        sl, lo, kw = head_place(n)
                        if sl != slot:
                            continue
                        for b in range(4):
                            last = nc.tensor.matmul(ps[lo:lo + kw, bank, b * V:(b + 1) * V],
                                                    skm[m % 2][:, b, lo:lo + kw],
                                                    val[0:NS, 4, n * V:(n + 1) * V], start=True, stop=True)
                    last.then_inc(s_kv, 1)

                for r in range(O_UNITS):
                    u = u0 + O0_UNIT + r
                    s = slot_of(u)
                    pe.wait_ge(lo_done, u + 1)
                    if h == 0 and r == 0:
                        pe.wait_ge(st_done, NSC)
                        pe.wait_ge(osq_act, 2 * NSC)
                    if h == 0 and r == 1:
                        pe.wait_ge(s_ln, 2)
                        pe.wait_ge(ln_act, 2 * NSC)
                    if h == 1 and r == 1:
                        pe.wait_ge(st_done, 2 * NSC)
                        pe.wait_ge(ln_act, 4 * NSC)
                        pe.wait_ge(osq_act, 4 * NSC)
                    if r >= 2:
                        pe.wait_ge(ev_v, u + 1)
                    turns = turns_at(h, r)
                    if h == 0 and r == 2:
                        pe.wait_ge(s_upd, 2 * SLOTS)
                    w_hi = whi[s][:].rearrange("p (k n) -> p k n", k=KT_D)
                    w_lo = wlo[s][:].rearrange("p (k n) -> p k n", k=KT_D)
                    for t, (_, rows, _) in enumerate(half_tiles(h)):
                        if r == 0:
                            pe.wait_ge(ol_dve, split_count(C0 + t) if t < 4 else NSC + 1)
                        o = ps[:, 4 * (u % 2) + t // 2, 256 * (t % 2):256 * (t % 2 + 1)]
                        for k in range(NH):
                            if t < 4:
                                last = three(o, pr_main[:, t, GT + k, :], pr_main[:, t, k, :], w_hi[:, k, :],
                                             w_lo[:, k, :], k == 0, k == NH - 1)
                            else:
                                last = both(o, pr_att[:, k].rearrange("p e t -> p (e t)"), w_hi[:, k, :], w_lo[:, k, :],
                                            k == 0, k == NH - 1)
                        if t == len(half_tiles(h)) - 1:
                            last.then_inc(used, 1)
                        if h == 0 and r < 2:
                            if r == 0 and t == 1:
                                pe.wait_ge(s_osq, 2)
                                for g in range(2):
                                    last = nc.tensor.matmul(
                                        ps[:, g, 4 * NS:8 * NS].rearrange("p (n t) -> p n t", n=4),
                                        ones, sum_place(0, g, True), start=True, stop=True)
                                last.then_inc(s_ss, 1)
                            for _ in range(S_PIECES[r][t]):
                                sample_piece(m)
                                m += 1
                        if t < 4 and turns[t] is not None:
                            turn(h + 1, turns[t])

            w1_hi, w3_hi = (whi[s][:].rearrange("p (k n) -> p k n", k=KT_D) for s in range(2))
            w1_lo, w3_lo = (wlo[s][:].rearrange("p (k n) -> p k n", k=KT_D) for s in range(2))
            w2_hi = whi[2][:].rearrange("p (k n) -> p k n", k=2)
            w2_lo = wlo[2][:].rearrange("p (k n) -> p k n", k=2)

            def w1_step(st):
                ch, ft = divmod(st, 2)
                col, w = FF_CHUNKS[ch]
                a, b = slice(ft * P, (ft + 1) * P), slice(col, col + w)
                for k in range(KT_D):
                    three(ps[:, 2 * (st % 2), 0:w], w1_hi[:, k, a], w1_lo[:, k, a], f_hi[:, k, b], f_lo[:, k, b],
                          k == 0, k == KT_D - 1)

            def w3_step(st, first=0, end=KT_D):
                ch, ft = divmod(st, 2)
                col, w = FF_CHUNKS[ch]
                a, b = slice(ft * P, (ft + 1) * P), slice(col, col + w)
                for k in range(first, end):
                    last = three(ps[:, 2 * (st % 2) + 1, 0:w], w3_hi[:, k, a], w3_lo[:, k, a],
                                 f_hi[:, k, b], f_lo[:, k, b], k == 0, k == KT_D - 1)
                if end == KT_D:
                    last.then_inc(step_pe, 1)

            def hidden(i, steps):
                for st in steps:
                    pe.wait_ge(gl_done, i * 6 + (st + 1))
                    w1_step(st)
                    w3_step(st)

            def outputs(i):
                pe.wait_ge(lo_done, i * 3 + (F0_UNIT + 3))
                for n, t in enumerate(OUT_TILES):
                    if n % 3 == 0:
                        pe.wait_ge(gl_done, i * 6 + (2 * (n // 3) + 4))
                    for q in range(2):
                        m = 2 * n + q
                        pe.wait_ge(y_dve, i * 18 + (m + 1))
                        o = ps[:, 4 + m % 4, :]
                        for k in range(2):
                            b = slice(512 * q, 512 * (q + 1))
                            if t < 8:
                                a = slice(t * P, (t + 1) * P)
                                last = three(o, g_hi[:, k, a], g_lo[:, k, a], w2_hi[:, k, b], w2_lo[:, k, b],
                                             k == 0, k == 1)
                            else:
                                last = both(o, g_samp[:, k].rearrange("p e t -> p (e t)"), w2_hi[:, k, b], w2_lo[:, k, b],
                                            k == 0, k == 1)
                        last.then_inc(y_pe, 1)

            pe.wait_ge(lo_done, F0_UNIT + 1)
            pe.wait_ge(ev_v, F0_UNIT + 1)
            pe.wait_ge(tl_done, turns_before(3))
            w1_step(0)
            w1_step(1)
            pe.wait_ge(lo_done, F0_UNIT + 2)
            w3_step(0)
            pe.wait_ge(ev_v, F0_UNIT + 2)
            for k in range(4):
                turn(3, k)
            w3_step(1, 0, 3)
            for k in range(4, KT_D):
                turn(3, k)
            w3_step(1, 3)
            pe.wait_ge(tl_done, turns_before(N_STAGES))
            hidden(0, range(2, 6))
            outputs(0)
            with pe.Fori(1, GROUPS - 1) as i:
                pe.wait_ge(lo_done, i * 3 + (F0_UNIT + 2))
                hidden(i, range(6))
                outputs(i)
            pe.wait_ge(lo_done, (GROUPS - 1) * 3 + (F0_UNIT + 2))
            hidden(GROUPS - 1, range(6))
            outputs(GROUPS - 1)


def _layout(inputs):
    import numpy as np

    f = {k: np.asarray(v) for k, v in inputs.items()}
    w_in = f["w_in"][0]
    starts = np.cumsum([0, HA * KA, HA * KA, HA * V, HA * V, RANK, HB * P, HB * P, HB * V])
    qa, ka, va, ga, lra, qb, fb, ib, gb = (int(s) for s in starts)

    def unit(w, rows, first, cols):
        part = w[:, first:first + cols]
        return np.ascontiguousarray(part.reshape(rows // P, P, cols).transpose(1, 0, 2)).reshape(P, -1)

    gate = [w_in[:, c + V * m:c + V * (m + 1)] for c, m in
            [(ga, n) if n < HA else (gb, n - HA) for n in ORDER]]
    wstream_a = np.stack([unit(w_in, D, c, 256) for c in (qa, qb, qb + 256, ka, fb, fb + 256)]
                         + [unit(np.concatenate(gate[m:m + 2], axis=1), D, 0, 256) for m in range(0, NH, 2)])
    low = w_in[:, lra:lra + RANK].reshape(KT_D, P, RANK).transpose(1, 0, 2)
    low = np.concatenate([low, low], axis=2)
    v_cols = [va, va + 256, ib, ib + 256]
    w_o = f["w_o"][0].reshape(NH, V, D)[ORDER].reshape(NH * V, D)
    wstream_b = np.stack([unit(w_in, D, c, 256) for c in v_cols] + [unit(w_o, D, 256 * j, 256) for j in range(4)])
    w1, w3, w2 = f["w1"][0], f["w3"][0], f["w2"][0]
    wstream_f = np.stack([part for i in range(GROUPS) for part in (
        unit(w1, D, 256 * i, 256), unit(w3, D, 256 * i, 256), unit(w2[256 * i:256 * (i + 1)], 256, 0, D))])

    consts = np.zeros((P, C_ALL), np.float32)
    pos = np.arange(SC)
    consts[:, C_ID:C_ID + P] = np.eye(P)
    consts[:, C_ONE:C_ONE + P] = 1
    consts[:, C_CAUSAL:C_CAUSAL + P] = pos[:, None] <= pos[None, :]
    consts[:, C_M32:C_M32 + SLOTS * SC] = np.tile(pos % CH != 0, SLOTS)
    tok = np.arange(NS)
    consts[:, C_M8:C_M8 + SLOTS * NS] = np.tile(tok % ST != 0, SLOTS)
    same = tok[:, None] // ST == tok[None, :] // ST
    consts[0:NS, C_SMASK:C_SMASK + NS] = same & (tok[:, None] <= tok[None, :])
    consts[0:NS, C_BMASK:C_BMASK + SB] = tok[:, None] // ST == np.arange(SB)[None, :]

    def cols(v):
        return v.reshape(-1, P).T

    pvec = np.concatenate([cols(f["norm_mix"][0]), cols(f["norm_ffn"][0]), cols(f["b_a"][0]),
                           cols(f["lb_param"][0]), cols(f["lb_param"][1]), cols(f["onorm_a"][0]),
                           cols(f["onorm_b"][0])], axis=1)
    arrays = {
        "x_prompt": f["x_prompt"][0], "x_sample": f["x_sample"].reshape(NS, D),
        "state_gla": f["state_gla"][0], "state_hgrn": f["state_hgrn"][0],
        "wstream_a": wstream_a, "wstream_l": low.reshape(P, -1), "wstream_b": wstream_b, "wstream_f": wstream_f,
        "consts": consts, "pvec": pvec, "w_a2": f["w_a2"][0], "norm_final": f["norm_final"],
    }
    return {k: np.ascontiguousarray(v) for k, v in arrays.items()}


_OUTS = [("y_prompt", (SEQ, D)), ("y_sample", (NS, D)),
         ("new_gla_p", (HA, KA, V)), ("new_hgrn_p", (HB, P, V)),
         ("new_gla_s", (SB, HA, KA, V)), ("new_hgrn_s", (SB, HB, P, V))]


def kernel(**inputs):
    import concourse.bacc as bacc
    from concourse.bass_utils import run_bass_kernel_spmd

    nc = bacc.Bacc("TRN2", target_bir_lowering=False, num_devices=1)
    arrays = _layout(inputs)
    args = [nc.dram_tensor(f"in_{k}", a.shape, mybir.dt.from_np(a.dtype), kind="ExternalInput").ap()
            for k, a in arrays.items()]
    args += [nc.dram_tensor(f"out_{k}", s, F32, kind="ExternalOutput").ap() for k, s in _OUTS]
    build(nc, *args)
    r = run_bass_kernel_spmd(nc, [{f"in_{k}": a for k, a in arrays.items()}], core_ids=[0]).results[0]
    y_p, y_s, gla_p, hgrn_p, gla_s, hgrn_s = (r[f"out_{k}"] for k, _ in _OUTS)
    return (y_p.reshape(1, SEQ, D), y_s.reshape(SB, ST, D), gla_p[None, None], hgrn_p[None, None],
            gla_s[None], hgrn_s[None])
```
